# Optimizing a Trainium2 kernel written in Bass

```python
import math
import jax
import jax.numpy as jnp
from jax import lax
import numpy as np

D_MODEL = 1024
BATCH = 1
SEQ = 512
DEPTH = 2

CHUNK = 64
NORM_EPS = 1e-6
L2_EPS = 1e-6
D_FF = 2816
MACARON_WEIGHT = 0.5
DN_HEADS = 4
DN_HEAD_DIM = 128
DN_WIDTH = DN_HEADS * DN_HEAD_DIM
CONV_K = 4
SWA_Q_HEADS = 8
SWA_KV_HEADS = 2
SWA_GROUP = SWA_Q_HEADS // SWA_KV_HEADS
SWA_HEAD_DIM = 64
SWA_Q_WIDTH = SWA_Q_HEADS * SWA_HEAD_DIM
SWA_KV_WIDTH = SWA_KV_HEADS * SWA_HEAD_DIM
SWA_WINDOW = 128
WINDOW_CHUNKS = SWA_WINDOW // CHUNK
ROPE_THETA = 10000.0
MIX_SPLIT_SIZES = (DN_WIDTH, DN_WIDTH, DN_WIDTH, DN_WIDTH, DN_HEADS, DN_HEADS,
                   SWA_Q_WIDTH, SWA_KV_WIDTH, SWA_KV_WIDTH, D_MODEL, D_MODEL)
MIX_IN_WIDTH = sum(MIX_SPLIT_SIZES)

kernel_name = "hybrid_gdn_swa_macaron_block"

def rms_norm(x, gain):
    xf = x.astype(jnp.float32)
    y = xf * lax.rsqrt(jnp.mean(xf * xf, axis=-1, keepdims=True) + NORM_EPS)
    return (y * gain.astype(jnp.float32)).astype(x.dtype)

def l2_norm(x):
    return x * lax.rsqrt(jnp.sum(x * x, axis=-1, keepdims=True) + L2_EPS)

def swiglu(u, w_in, w_out):
    gate, up = jnp.split(u @ w_in, 2, axis=-1)
    return (jax.nn.silu(gate) * up) @ w_out

def causal_depthwise_conv(x, w):
    k = w.shape[0]
    s = x.shape[1]
    xp = jnp.pad(x, ((0, 0), (k - 1, 0), (0, 0)))
    return sum(xp[:, j:j + s] * w[j] for j in range(k))

def apply_rope(t, cos, sin):
    half = t.shape[-1] // 2
    tf = t.astype(jnp.float32)
    t1, t2 = tf[..., :half], tf[..., half:]
    c = cos[None, :, None, :]
    s_ = sin[None, :, None, :]
    return jnp.concatenate([t1 * c - t2 * s_, t2 * c + t1 * s_], axis=-1)

def to_chunks(t, n):
    b = t.shape[0]
    return jnp.moveaxis(t.reshape((b, n, CHUNK) + t.shape[2:]), 3, 2)

def gated_delta_rule(q, k, v, g, beta):
    b, s, h, dk = q.shape
    dv = v.shape[-1]
    n = s // CHUNK
    qc = to_chunks(q * dk ** -0.5, n)
    kc = to_chunks(k, n)
    vc = to_chunks(v, n)
    gc = jnp.cumsum(to_chunks(g, n), axis=-1)
    bc = to_chunks(beta, n)
    idx = jnp.arange(CHUNK)
    causal = idx[:, None] >= idx[None, :]
    strict = idx[:, None] > idx[None, :]
    decay = jnp.exp(jnp.where(causal, gc[..., :, None] - gc[..., None, :], -jnp.inf))
    k_beta = kc * bc[..., None]
    v_beta = vc * bc[..., None]
    lower = jnp.where(strict, jnp.einsum('bnhid,bnhjd->bnhij', k_beta, kc) * decay, 0.0)
    a_mat = jnp.eye(CHUNK, dtype=jnp.float32) + lower
    rhs = jnp.concatenate([v_beta, k_beta * jnp.exp(gc)[..., None]], axis=-1)
    sol = lax.linalg.triangular_solve(a_mat, rhs, left_side=True, lower=True, unit_diagonal=True)
    u_c, w_c = sol[..., :dv], sol[..., dv:]
    attn_qk = jnp.einsum('bnhid,bnhjd->bnhij', qc, kc) * decay

    def step(state, inp):
        q_i, k_i, u_i, w_i, g_i, a_i = inp
        v_new = u_i - jnp.einsum('bhcd,bhde->bhce', w_i, state)
        o = (jnp.einsum('bhcd,bhde->bhce', q_i * jnp.exp(g_i)[..., None], state)
             + jnp.einsum('bhij,bhje->bhie', a_i, v_new))
        g_last = g_i[..., -1]
        state = (state * jnp.exp(g_last)[..., None, None]
                 + jnp.einsum('bhcd,bhce->bhde', k_i * jnp.exp(g_last[..., None] - g_i)[..., None], v_new))
        return state, o

    xs = tuple(jnp.moveaxis(t, 1, 0) for t in (qc, kc, u_c, w_c, gc, attn_qk))
    _, o = lax.scan(step, jnp.zeros((b, h, dk, dv), jnp.float32), xs)
    o = jnp.moveaxis(jnp.moveaxis(o, 0, 1), 2, 3)
    return o.reshape(b, s, h, dv)

def deltanet_branch(q, k, v, z, beta_logit, alpha_logit, conv_w, a_log, dt_bias, out_norm):
    b, s, _ = q.shape
    qkv = jax.nn.silu(causal_depthwise_conv(jnp.concatenate([q, k, v], axis=-1), conv_w))
    qkv = qkv.astype(jnp.float32).reshape(b, s, 3, DN_HEADS, DN_HEAD_DIM)
    qh = l2_norm(qkv[:, :, 0])
    kh = l2_norm(qkv[:, :, 1])
    vh = qkv[:, :, 2]
    beta = jax.nn.sigmoid(beta_logit.astype(jnp.float32))
    g = -jnp.exp(a_log.astype(jnp.float32)) * jax.nn.softplus(
        alpha_logit.astype(jnp.float32) + dt_bias.astype(jnp.float32))
    o = gated_delta_rule(qh, kh, vh, g, beta)
    zh = z.astype(jnp.float32).reshape(b, s, DN_HEADS, DN_HEAD_DIM)
    o = rms_norm(o, out_norm) * jax.nn.silu(zh)
    return o.reshape(b, s, DN_WIDTH)

def swa_sink_branch(q, k, v, sinks, cos, sin):
    b, s, _ = q.shape
    n = s // CHUNK
    qh = apply_rope(q.reshape(b, s, SWA_Q_HEADS, SWA_HEAD_DIM), cos, sin)
    kh = apply_rope(k.reshape(b, s, SWA_KV_HEADS, SWA_HEAD_DIM), cos, sin)
    vh = v.astype(jnp.float32).reshape(b, s, SWA_KV_HEADS, SWA_HEAD_DIM)
    pad = (WINDOW_CHUNKS - 1) * CHUNK
    kp = jnp.pad(kh, ((0, 0), (pad, 0), (0, 0), (0, 0)))
    vp = jnp.pad(vh, ((0, 0), (pad, 0), (0, 0), (0, 0)))
    kb = jnp.concatenate([kp[:, j * CHUNK:j * CHUNK + s].reshape(b, n, CHUNK, SWA_KV_HEADS, SWA_HEAD_DIM)
                          for j in range(WINDOW_CHUNKS)], axis=2)
    vb = jnp.concatenate([vp[:, j * CHUNK:j * CHUNK + s].reshape(b, n, CHUNK, SWA_KV_HEADS, SWA_HEAD_DIM)
                          for j in range(WINDOW_CHUNKS)], axis=2)
    qb = qh.reshape(b, n, CHUNK, SWA_KV_HEADS, SWA_GROUP, SWA_HEAD_DIM)
    scores = jnp.einsum('bnqkgd,bnjkd->bnkgqj', qb, kb) * SWA_HEAD_DIM ** -0.5
    chunk_ids = jnp.arange(n)[:, None] - (WINDOW_CHUNKS - 1) + jnp.arange(WINDOW_CHUNKS)[None, :]
    key_valid = jnp.repeat(chunk_ids >= 0, CHUNK, axis=1)
    scores = jnp.where(key_valid[None, :, None, None, None, :], scores, -jnp.inf)
    sink = sinks.astype(jnp.float32).reshape(SWA_KV_HEADS, SWA_GROUP)[None, None, :, :, None, None]
    m = jnp.maximum(jnp.max(scores, axis=-1, keepdims=True), sink)
    p = jnp.exp(scores - m)
    probs = p / (jnp.sum(p, axis=-1, keepdims=True) + jnp.exp(sink - m))
    out = jnp.einsum('bnkgqj,bnjkd->bnqkgd', probs, vb)
    return out.reshape(b, s, SWA_Q_WIDTH)

def setup_inputs(seed: int = 0) -> dict:
    key = jax.random.key(seed)
    ks = jax.random.split(key, 24)
    f32 = jnp.float32

    def dense(k, fan_in, fan_out):
        return jax.random.normal(k, (DEPTH, fan_in, fan_out), f32) * fan_in ** -0.5

    def gain(k, n):
        return 1.0 + 0.02 * jax.random.normal(k, (DEPTH, n), f32)

    dt = jnp.exp(jax.random.uniform(ks[10], (DEPTH, DN_HEADS), f32, math.log(1e-3), math.log(1e-1)))
    return {
        "x": jax.random.normal(ks[0], (BATCH, SEQ, D_MODEL), f32),
        "ffn1_pre_norm": gain(ks[1], D_MODEL),
        "ffn1_w_in": dense(ks[2], D_MODEL, 2 * D_FF),
        "ffn1_w_out": dense(ks[3], D_FF, D_MODEL),
        "ffn1_post_norm": gain(ks[4], D_MODEL),
        "mix_pre_norm": gain(ks[5], D_MODEL),
        "mix_w_in": dense(ks[6], D_MODEL, MIX_IN_WIDTH),
        "dn_conv_w": jax.random.normal(ks[7], (DEPTH, CONV_K, 3 * DN_WIDTH), f32) * CONV_K ** -0.5,
        "dn_a_log": jnp.log(jax.random.uniform(ks[8], (DEPTH, DN_HEADS), f32, 1.0, 16.0)),
        "dn_dt_bias": dt + jnp.log(-jnp.expm1(-dt)),
        "dn_out_norm": gain(ks[9], DN_HEAD_DIM),
        "swa_sinks": jax.random.normal(ks[11], (DEPTH, SWA_Q_HEADS), f32),
        "w_branch_a": dense(ks[12], DN_WIDTH, D_MODEL),
        "w_branch_b": dense(ks[13], SWA_Q_WIDTH, D_MODEL),
        "mix_w_out": dense(ks[14], D_MODEL, D_MODEL),
        "mix_post_norm": gain(ks[15], D_MODEL),
        "ffn2_pre_norm": gain(ks[16], D_MODEL),
        "ffn2_w_in": dense(ks[17], D_MODEL, 2 * D_FF),
        "ffn2_w_out": dense(ks[18], D_FF, D_MODEL),
        "ffn2_post_norm": gain(ks[19], D_MODEL),
    }

def reference(x, ffn1_pre_norm, ffn1_w_in, ffn1_w_out, ffn1_post_norm, mix_pre_norm, mix_w_in,
              dn_conv_w, dn_a_log, dn_dt_bias, dn_out_norm, swa_sinks, w_branch_a, w_branch_b,
              mix_w_out, mix_post_norm, ffn2_pre_norm, ffn2_w_in, ffn2_w_out, ffn2_post_norm):
    s = x.shape[1]
    half = SWA_HEAD_DIM // 2
    inv_freq = ROPE_THETA ** (-jnp.arange(half, dtype=jnp.float32) / half)
    ang = jnp.arange(s, dtype=jnp.float32)[:, None] * inv_freq[None, :]
    cos, sin = jnp.cos(ang), jnp.sin(ang)
    split_points = [int(p) for p in np.cumsum(MIX_SPLIT_SIZES)[:-1]]
    for l in range(DEPTH):
        x = x + MACARON_WEIGHT * rms_norm(
            swiglu(rms_norm(x, ffn1_pre_norm[l]), ffn1_w_in[l], ffn1_w_out[l]), ffn1_post_norm[l])
        u = rms_norm(x, mix_pre_norm[l])
        (dq, dk, dv, dz, db, da, sq, sk, sv, gate_a, gate_b) = jnp.split(u @ mix_w_in[l], split_points, axis=-1)
        y_a = deltanet_branch(dq, dk, dv, dz, db, da, dn_conv_w[l], dn_a_log[l], dn_dt_bias[l],
                              dn_out_norm[l]).astype(x.dtype)
        y_b = swa_sink_branch(sq, sk, sv, swa_sinks[l], cos, sin).astype(x.dtype)
        merged = (jax.nn.sigmoid(gate_a) * (y_a @ w_branch_a[l])
                  + jax.nn.sigmoid(gate_b) * (y_b @ w_branch_b[l]))
        x = x + rms_norm(merged @ mix_w_out[l], mix_post_norm[l])
        x = x + MACARON_WEIGHT * rms_norm(
            swiglu(rms_norm(x, ffn2_pre_norm[l]), ffn2_w_in[l], ffn2_w_out[l]), ffn2_post_norm[l])
    return x


_drawn_inputs = setup_inputs


def setup_inputs(seed=0):
    import zlib

    import numpy as np

    out = dict(_drawn_inputs(seed))
    spreads = {}
    factors = {'ffn1_post_norm': 2.955,
     'dn_out_norm': 8.839,
     'swa_sinks': 8.0,
     'ffn2_pre_norm': 4.145,
     'ffn2_post_norm': 16.281,
     'mix_post_norm': 3.0}
    for name, (base, spread) in spreads.items():
        noise = np.random.default_rng([zlib.crc32(name.encode()), seed]).standard_normal(out[name].shape)
        drawn = base * np.exp(spread * noise) if base else spread * noise
        out[name] = jnp.asarray(drawn.astype(out[name].dtype))
    for name, factor in factors.items():
        out[name] = (out[name] * factor).astype(out[name].dtype)
    return out
```

```python
import concourse.bass as bass
from concourse import mybir
from contextlib import ExitStack

DEPTH, SEQ, D, FF = 2, 512, 1024, 2816
P = 128
KT = D // P
FT = FF // P
TT = SEQ // P
CH = 64
NCH = SEQ // CH
H = 4
EPS = 1e-6
DK_SCALE = float(P) ** -0.5
SWA_SCALE = float(CH) ** -0.5
RING = 4

A_CHUNKS = (FT // 2) * (KT // 2)
B_CHUNKS = 24
M_CHUNKS = 56
LAYER_CHUNKS = 2 * (A_CHUNKS + B_CHUNKS) + M_CHUNKS
CHUNK_A = (0, A_CHUNKS + B_CHUNKS + M_CHUNKS)
CHUNK_M = A_CHUNKS + B_CHUNKS
M_UNITS = 36 * 4 + 4 * 2 + 16 * 4
LAYER_UNITS = 2 * 4 * (A_CHUNKS + B_CHUNKS) + M_UNITS
UNIT_A = (0, 4 * (A_CHUNKS + B_CHUNKS) + M_UNITS)
UNIT_M = 4 * (A_CHUNKS + B_CHUNKS)
M_TILES = 38 + 16 + 8
FFN_TILES = 2 * FT + KT
LAYER_TILES = 2 * FFN_TILES + M_TILES
TILE_A = (0, FFN_TILES + M_TILES)
TILE_M = FFN_TILES
HALVES = range(16, 20)


def out_ks(i):
    return (i,) if i < 2 else (2 * i - 2, 2 * i - 1)


def m_unit(j):
    return UNIT_M + (4 * j if j < 16 else 64 + 2 * (j - 16) if j < 20 else 72 + 4 * (j - 20))


G_PRE, G_POST = (0, 16), (8, 24)
G_MIXPRE, G_MIXPOST = 32, 40
C_CONV = 48
C_ONORM = 96
C_ALOG, C_DT, C_SINK = 97, 101, 105
C_BA = 109
NPAR = C_BA + 64

K_ID, K_ONE, K_TRI, K_STRICT, K_ROT, K_SELA, K_SELB = (P * i for i in range(7))
K_S64 = 7 * P
K_I64, K_TRI64, K_STR64 = K_S64, K_S64 + 64, K_S64 + 128
K_LEV = K_S64 + 192
LEVELS = 6
NCONST = K_LEV + 64 * LEVELS


def mix_steps():
    s = {j: [] for j in range(M_CHUNKS)}
    s[3] = [("xnorm",), ("evac", 0), ("evac", 1), ("evac", 2), ("ba",), ("evac", 3), ("conv", 0)]
    s[4] = [("bat",), ("gprep",), ("silu", 0), ("conv", 1)]
    s[5] = [("gsum",), ("conv", 2), ("silu", 1)]
    s[6] = [("lst", 0, 0), ("conv", 3), ("silu", 2), ("decay", 0), ("decay", 1)]
    s[7] = [("evac", 4), ("evac", 5), ("evac", 6), ("evac", 7), ("lst", 0, 1), ("silu", 3), ("conv", 4)]
    s[8] = [("lst", 0, 2), ("lst", 0, 3), ("lpow", 0), ("conv", 5), ("silu", 4)]
    s[9] = [("conv", 6), ("silu", 5), ("row", 0, 0), ("row", 0, 1)]
    s[10] = [("conv", 7), ("silu", 6), ("row", 0, 2), ("row", 0, 3)]
    s[11] = [("evac", 8), ("evac", 9), ("evac", 10), ("evac", 11), ("silu", 7), ("conv", 8), ("kk", 0), ("kk", 1)]
    s[12] = [("conv", 9), ("silu", 8), ("inv1", 0), ("inv1", 1), ("ktr", 0), ("ktr", 1)]
    s[13] = [("conv", 10), ("silu", 9), ("lst", 1, 0), ("invp", 0, 1), ("invp", 1, 1), ("ktr", 2), ("ktr", 3)]
    s[14] = [("conv", 11), ("silu", 10), ("lst", 1, 1), ("invd", 0, 1), ("invd", 1, 1)]
    s[15] = [("evac", 12), ("evac", 13), ("evac", 14), ("evac", 15), ("silu", 11), ("lst", 1, 2),
             ("invp", 0, 2), ("invp", 1, 2), ("vtr", 0), ("vtr", 1)]
    s[16] = [("lst", 1, 3), ("lpow", 1), ("rope", 0), ("rope", 1), ("invd", 0, 2), ("invd", 1, 2)]
    s[17] = [("rope", 2), ("rope", 3), ("invp", 0, 3), ("invp", 1, 3), ("vtr", 2), ("vtr", 3)]
    s[18] = [("row", 1, 0), ("row", 1, 1), ("invd", 0, 3), ("invd", 1, 3), ("row", 1, 2)]
    s[19] = [("evac", 16), ("evac", 17), ("row", 1, 3), ("invp", 0, 4), ("invp", 1, 4), ("rope", 4)]
    s[20] = [("invd", 0, 4), ("invd", 1, 4), ("vwin", 0), ("vwin", 1)]
    s[21] = [("invp", 0, 5), ("invp", 1, 5), ("qk", 0), ("qk", 1)]
    s[22] = [("invd", 0, 5), ("invd", 1, 5), ("sc", 0), ("grow", 0), ("grow", 1)]
    s[23] = [("evac", i) for i in range(18, 22)] + [("wt", t) for t in range(TT)] + [("grow", 2), ("grow", 3)]
    for n in range(NCH):
        if n:
            s[22 + n].append(("sc", n))
        s[23 + n].append(("pt", n))
        s[24 + n].append(("pv", n))
        s[24 + 2 * n].append(("sv", n))
        s[25 + 2 * n].append(("so", n))
    for i in range(4):
        s[24 + i].append(("zsilu", i))
    for g in range(4):
        s[27 + 4 * g] = [("evac", 22 + 4 * g + i) for i in range(4)] + s[27 + 4 * g]
    s[39] += [("ybs", t) for t in range(4)]
    s[40] += [("ost", 0), ("ost", 1)]
    s[41] += [("evac", 38 + i) for i in range(4)] + [("ost", 2), ("ost", 3), ("opow",)]
    s[42] += [("orow", 0), ("orow", 1)]
    for b, j in enumerate((43, 45, 47)):
        s[j] += [("evac", 42 + 4 * b + i) for i in range(4)]
    s[43] = s[43][:-2] + [("orow", 2)] + s[43][-2:] + [("orow", 3)]
    return s


MIX_STEPS = mix_steps()


def banks_of(step):
    k, x = step[0], (step[1] if len(step) > 1 else 0)
    if k in ("ba", "bat", "gsum", "vwin", "sc"):
        return (5,)
    if k == "lst":
        return (5,) if step[2] == 0 else ()
    if k == "ost":
        return (5,) if x == 0 else ()
    if k == "decay":
        return (6 + x,)
    if k == "row":
        return (6 + step[2] % 2,) if x == 0 else (5,)
    if k == "orow":
        return (6 + x % 2,)
    if k == "kk":
        return (4 + x,)
    if k == "inv1":
        return (6 + x,)
    if k == "ktr":
        return (4,) if x < 2 else (7,)
    if k == "vtr":
        return (7,)
    if k == "invp":
        return (4,) if x == 0 else (6,)
    if k == "invd":
        if step[2] == LEVELS - 1:
            return (7,) if x == 0 else (4,)
        return (7, 4) if x == 0 else (6, 7)
    if k == "rope":
        return (2 + x % 2,) if x < 4 else (5,)
    if k == "qk":
        return (5,) if x == 0 else (7,)
    if k == "grow":
        return (6,)
    if k == "wt":
        return (4,) if x % 2 == 0 else (7,)
    if k == "pt":
        return (6,)
    if k == "pv":
        return (7,)
    if k == "sv":
        return (4,)
    if k == "so":
        return (7,) if x == NCH - 1 else (7, 4)
    return ()


def count_uses():
    seen, use = {b: 0 for b in (2, 3, 4, 5, 6, 7)}, {}
    for j in range(M_CHUNKS):
        for step in MIX_STEPS[j]:
            for b in banks_of(step):
                use[step, b] = seen[b]
                seen[b] += 1
    for w in (0, 1):
        for h in range(1, 4):
            use[("lst", w, h), 5] = use[("lst", w, 0), 5]
    for h in range(1, 4):
        use[("ost", h), 5] = use[("ost", 0), 5]
    return use, seen


USE, USES = count_uses()


def block_cols(v, lev, odd):
    s = 1 << lev
    names = " ".join("pabcd"[:len(v.shape) - 1])
    w = v.rearrange(f"{names} (n o s) -> {names} n o s", o=2, s=s)
    return w[:, :, odd, :] if len(v.shape) == 2 else w[:, :, :, odd, :]


def half_cols(v, lev):
    return v.rearrange("p (c n s) -> p c n s", c=8, s=1 << lev)


class Signal:

    def __init__(self, handle, per, grant=0):
        self.h, self.per, self.grant = handle, per, grant

    def at(self, layer, n):
        return layer * self.per + (n + self.grant)


def trunk(nc, wstream, xT, par, consts, rope, out):
    f32, f32r = mybir.dt.float32, mybir.dt.float32r
    ALU, ACT, AX = mybir.AluOpType, mybir.ActivationFunctionType, mybir.AxisListType
    ctx = ExitStack()
    with ctx:
        kb = 1024
        base = -(-nc.sbuf_base // 32) * 32
        top = nc.sbuf_usable_end

        def at(name, shape, off, dt=f32):
            return nc.alloc_sbuf_tensor_at(name, shape, dt, offset=base + int(off))

        X_AT, HHI_AT, HLO_AT = 0, 16 * kb, 60 * kb
        x = at("x", [P, KT, SEQ], X_AT)
        hhi = at("hhi", [P, FT, SEQ], HHI_AT, f32r)
        hlo = at("hlo", [P, FT, SEQ], HLO_AT, f32r)
        uhi = at("uhi", [P, KT, SEQ], 104 * kb, f32r)
        ulo = at("ulo", [P, KT, SEQ], 120 * kb, f32r)
        raw = at("raw", [P, RING, 1024], 136 * kb)
        whi = at("whi", [P, RING, 1024], 152 * kb, f32r)
        wlo = at("wlo", [P, RING, 1024], 168 * kb, f32r)
        tmp = at("tmp", [P, 6, SEQ], 184 * kb)
        rrow = at("rrow", [P, SEQ], 196 * kb)
        free = [198 * kb]

        def small(name, cols, dt=f32):
            off = free[0]
            free[0] += -(-cols // 8) * 32
            return at(name, [P, cols], off, dt)

        con = small("con", NCONST)
        prm = small("prm", (DEPTH + 1) * NPAR)
        bahi, balo = small("bahi", 64, f32r), small("balo", 64, f32r)
        ms, rc = small("ms", 16), small("rc", 16)
        rcx = small("rcx", 4)
        neghalf = small("neghalf", 16)
        ba = small("ba", 32)
        beta, g = small("beta", 16), small("g", 16)
        ga_t, gb_t = small("ga_t", 16), small("gb_t", 16)
        ealog = small("ealog", 4)
        exs = small("exs", 64)
        mx, mneg, sm, es, rden = (small(n, 8) for n in ("mx", "mneg", "sm", "es", "rden"))
        assert base + free[0] <= top, free[0]

        kq = at("kq", [P, 2, H, SEQ], 0)
        wneg = at("wneg", [P, H, SEQ], 0)
        vT = at("vT", [P, H, SEQ], 16 * kb)
        yb = at("yb", [P, H, SEQ], 16 * kb)
        vtm = at("vtm", [P, TT, H, P], 24 * kb)
        ktl = at("ktl", [P, TT, H, P], 32 * kb)
        attnT = at("attnT", [P, 16, CH], 40 * kb)
        Z = at("Z", [P, 16, CH], 44 * kb)
        S = at("S", [P, H, P], 48 * kb)
        vn = at("vn", [P, H, P], 50 * kb)
        N = at("N", [P, 16, CH], 52 * kb)
        Pm = at("Pm", [P, 16, CH], 56 * kb)
        Zt = at("Zt", [P, 16, CH], 60 * kb)
        Cs = at("Cs", [P, 16, CH], 64 * kb)
        E = at("E", [P, 16, CH], 68 * kb)
        oT = at("oT", [P, H, SEQ], 52 * kb)
        z = at("z", [P, H, SEQ], 60 * kb)
        kte = at("kte", [P, TT, H, P], 72 * kb)
        cv = at("cv", [P, 4, 516], 80 * kb)
        sq = at("sq", [P, NCH, 4, CH], 80 * kb)
        sk = at("sk", [P, SEQ], 88.5 * kb)
        vwin = at("vwin", [P, NCH, P], 90.5 * kb)
        sv = at("sv", [P, SEQ], 94.5 * kb)
        pexp = at("pexp", [P, 4, P], 94.5 * kb)
        pT = at("pT", [P, 4, P], 96.5 * kb)
        rcs = at("rcs", [P, 2, SEQ], 98.5 * kb)
        gates = at("gates", [P, 16, SEQ], 72 * kb)
        yahi = at("yahi", [P, 4, SEQ], 24 * kb, f32r)
        yalo = at("yalo", [P, 4, SEQ], 32 * kb, f32r)
        ybhi = at("ybhi", [P, 4, SEQ], 8 * kb, f32r)
        yblo = at("yblo", [P, 4, SEQ], 40 * kb, f32r)
        m1 = [at("m1a", [P, 4, SEQ], 0), at("m1b", [P, 4, SEQ], 16 * kb)]

        ps = ctx.enter_context(nc.psum_tensor("ps", [P, 8 * SEQ], f32))

        def bank(b, lo=0, n=SEQ, p0=0, p1=P):
            return ps[p0:p1, b * SEQ + lo:b * SEQ + lo + n]

        x_home = nc.dram_tensor("x_home", [P, KT, SEQ], f32).ap()

        def sem(name, per, grant=0):
            return Signal(ctx.enter_context(nc.semaphore(name)), per, grant)

        raw_ready = [sem(f"raw_ready{i}", LAYER_CHUNKS // RING * 16) for i in range(RING)]
        hi_done = sem("hi_done", LAYER_CHUNKS)
        split_done = sem("split_done", LAYER_CHUNKS, 4)
        gemm_done = sem("gemm_done", LAYER_UNITS, 16)
        tile_read = sem("tile_read", LAYER_TILES, 8)
        par_in, con_in = sem("par_in", 0), sem("con_in", 0)
        x_in = [sem(f"x_in{i}", 0) for i in range(4)]
        prepared = sem("prepared", 0)
        sq_done = sem("sq_done", 48, 8)
        y_added = sem("y_added", 21)
        x_added = sem("x_added", 21, 7)
        x_new = sem("x_new", 24)
        u_hi = sem("u_hi", 24, 8)
        u_lo = sem("u_lo", 24, 8)
        stat_done = sem("stat_done", 6)
        ms_done = sem("ms_done", 9)
        rc_done = sem("rc_done", 9)
        row_done = sem("row_done", 6)
        r_ready = sem("r_ready", 6)
        y7_out = sem("y7_out", 3)
        ff_tanh = sem("ff_tanh", 2 * FT)
        ff_silu = sem("ff_silu", 2 * FT)
        ff_h = sem("ff_h", 2 * FT)
        h_hi = sem("h_hi", 2 * FT)
        h_lo = sem("h_lo", 2 * FT)
        dve_link = sem("dve_link", DVE_LINKS)
        act_link = sem("act_link", ACT_LINKS)
        pool_link = sem("pool_link", POOL_LINKS)
        pe_begun, pool_begun = sem("pe_begun", 0), sem("pool_begun", 0)
        misc = {b: sem(f"misc{b}", USES[b]) for b in USES}
        misc_out = {b: sem(f"misc_out{b}", USES[b], 1) for b in USES}
        x_out = sem("x_out", 16)
        x_back = sem("x_back", 16)
        rope_in = sem("rope_in", 16)
        pad_zero = sem("pad_zero", 1)
        tap0 = sem("tap0", 12)
        conv_done = sem("conv_done", 12)
        c_tanh = sem("c_tanh", 12)
        silu_done = sem("silu_done", 12)
        l_sq = sem("l_sq", 12)
        l_stat = sem("l_stat", 12)
        g_act = sem("g_act", 1)
        g_dve = sem("g_dve", 3)
        ea_done = sem("ea_done", 1)
        gs_done = sem("gs_done", 1)
        ba_hi = sem("ba_hi", 1)
        ba_lo = sem("ba_lo", 1)
        dmask = sem("dmask", 2)
        c_done = sem("c_done", 2 * LEVELS)
        p_zero = sem("p_zero", 2 * LEVELS - 2)
        z1_done = sem("z1_done", 2)
        rot_cos = sem("rot_cos", 5)
        roped = sem("roped", 5)
        row_exp = sem("row_exp", 4)
        q_e = sem("q_e", 4)
        w_half = sem("w_half", 4)
        sc_half = sem("sc_half", 8)
        sc_max = sem("sc_max", 8)
        p_norm = sem("p_norm", 8)
        es_done = sem("es_done", 8)
        s_new = sem("s_new", 7)
        z_tanh = sem("z_tanh", 4)
        z_done = sem("z_done", 4)
        gate_done = sem("gate_done", 16)
        ys_hi = sem("ys_hi", 8)
        ys_lo = sem("ys_lo", 8)
        o_done = sem("o_done", 4)
        mg_done = sem("mg_done", 8)
        mg_hi = sem("mg_hi", 8)
        mg_lo = sem("mg_lo", 8)
        out_done = sem("out_done", 0)

        ident, ones = con[:, K_ID:K_ID + P], con[:, K_ONE:K_ONE + P]
        tri, strict = con[:, K_TRI:K_TRI + P], con[:, K_STRICT:K_STRICT + P]
        i64 = con[:, K_I64:K_I64 + 64]

        def chunks(v):
            return v.rearrange("p (n c) -> p n c", c=CH)

        def attn_in(i):
            return sq[:, :, i, :] if i < 4 else chunks(sk[:, :])

        def many(v, n):
            return v.rearrange("p (a c) -> p a c", a=1).to_broadcast([P, n, 64])

        def pc(layer, col, n=1):
            return prm[:, bass.ds(layer * NPAR + col, n)]

        STAT = {"x0": 0, "y0": 1, "x1": 2, "k": 3, "q": 4, "o": 5, "y1": 6, "x2": 7, "y2": 8}
        ROW = {"x0": 0, "y0": 1, "x1": 2, "y1": 3, "x2": 4, "y2": 5}

        block = ctx.enter_context(nc.Block())

        @block.sync
        def _(sp):
            sp.dma_start(prm[:, :], par).then_inc(par_in.h, 16)
            for i in range(4):
                sp.dma_start(x[:, 2 * i:2 * i + 2, :], xT[:, 2 * i:2 * i + 2, :]).then_inc(x_in[i].h, 16)
                if i < 3:
                    sp.wait_ge(split_done.h, i + 1)
                    sp.dma_start(raw[:, i, :], wstream[i]).then_inc(raw_ready[i].h, 16)
            sp.dma_start(con[:, :], consts).then_inc(con_in.h, 16)

            def load(L, c, cols=1024, s=0):
                s = (s + 3) % RING
                sp.wait_ge(split_done.h, L * LAYER_CHUNKS + (c + 3 + 1))
                sp.dma_start(raw[:, s, 0:cols], wstream[L * LAYER_CHUNKS + (c + 3)][:, 0:cols]).then_inc(raw_ready[s].h, 16)

            def ffn(L, f):
                with sp.Fori(0, FT // 2) as it:
                    for s in range(4):
                        load(L, it * 4 + (CHUNK_A[f] + s), s=s)
                for i in range(B_CHUNKS):
                    load(L, CHUNK_A[f] + A_CHUNKS + i, 512 if i + 3 in (12, 13) else 1024, s=i % RING)

            with sp.Fori(0, DEPTH) as L:
                ffn(L, 0)
                for j in range(M_CHUNKS):
                    load(L, CHUNK_M + j, 512 if j + 3 in HALVES else 1024, s=j % RING)
                ffn(L, 1)
            for k in range(KT):
                sp.wait_ge(x_new.h, DEPTH * 24 - KT + k + 1)
                sp.dma_start(out[:, k, :], x[:, k, :]).then_inc(out_done.h, 16)
            sp.wait_ge(out_done.h, 16 * KT)

        @block.tensor
        def _(pe):
            pe.sem_inc(gemm_done.h, 16)

            def mm3(o, s, w, bhi, blo, first, last):
                lh, ll = whi[:, s, w * P:(w + 1) * P], wlo[:, s, w * P:(w + 1) * P]
                pe.matmul(o, lh, bhi, start=first, stop=False)
                pe.matmul(o, lh, blo, start=False, stop=False)
                return pe.matmul(o, ll, bhi, start=False, stop=last)

            def first_chunk(L, c, s, outs, u0, bank_free):
                pe.wait_ge(split_done.h, split_done.at(L, c + 1))
                for i in range(2):
                    pe.wait_ge(u_lo.h, u_lo.at(L, u0 + 2 * s + i + 1))
                    for m, o in enumerate(outs):
                        if s == 0 and i == 0:
                            pe.wait_ge(tile_read.h, tile_read.at(L, bank_free + m + 1))
                        k = 2 * s + i
                        last = mm3(o, s, i * len(outs) + m, uhi[:, k, :], ulo[:, k, :], k == 0, k == KT - 1)
                        if i:
                            last.then_inc(gemm_done.h, 1)

            def chunk(L, c, s, outs, ks, bhi, blo, k0, kn, before=None):
                pe.wait_ge(split_done.h, split_done.at(L, c + 1))
                for m, o in enumerate(outs):
                    if before is not None:
                        before(m)
                    for i, k in enumerate(ks):
                        last = mm3(o, s, i * len(outs) + m, bhi[:, k, :], blo[:, k, :], k == k0, k == kn - 1)
                    last.then_inc(gemm_done.h, 1)

            def stat(acc, o):
                for t in range(TT):
                    last = pe.matmul(o[:, t:t + 1], acc[:, t * P:(t + 1) * P], ones[:, 0:1], start=True, stop=True)
                return last

            def row(r, o):
                for t in range(TT):
                    last = pe.matmul(o[:, t * P:(t + 1) * P], r[:, t:t + 1].to_broadcast([P, P]), ident, start=True, stop=True)
                return last

            def x_stat(L, n):
                pe.wait_ge(con_in.h, 16)
                pe.wait_ge(x_added.h, x_added.at(L, 7 * n))
                stat(tmp[:, 5, :], bank(7)).then_inc(stat_done.h, 1)

            def x_row(L, n):
                pe.wait_ge(rc_done.h, rc_done.at(L, STAT[f"x{n}"] + 1))
                row(rcx, bank(7)).then_inc(row_done.h, 1)

            def y_norm(L, n):
                pe.wait_ge(y_added.h, y_added.at(L, 7 * n + 7))
                pe.wait_ge(y7_out.h, y7_out.at(L, n + 1))
                stat(tmp[:, 2, :], bank(7)).then_inc(stat_done.h, 1)
                pe.wait_ge(rc_done.h, rc_done.at(L, STAT[f"y{n}"] + 1))
                row(rc, bank(7)).then_inc(row_done.h, 1)

            def ffn(L, f):
                def group_in(it, odd, norm=False):
                    for s in range(4):
                        def before(m, s=s):
                            if s == 0:
                                if norm and m == 0:
                                    pe.wait_ge(tile_read.h, tile_read.at(L, TILE_A[f]))
                                    x_stat(L, 2 * f)
                                if norm and m == 2:
                                    x_row(L, 2 * f)
                                if norm and m == 3:
                                    pe.wait_ge(r_ready.h, r_ready.at(L, ROW[f"x{2 * f}"] + 1))
                                elif not (norm and m == 0):
                                    pe.wait_ge(tile_read.h, tile_read.at(L, it * 4 + (TILE_A[f] - 8 + m + 1)))
                        chunk(L, it * 4 + (CHUNK_A[f] + s), s, [bank(4 * odd + m) for m in range(4)], (2 * s, 2 * s + 1),
                              uhi, ulo, 0, KT, before)

                for s in range(4):
                    first_chunk(L, CHUNK_A[f] + s, s, [bank(m) for m in range(4)], 16 * f - 8, TILE_A[f] - 8)
                group_in(1, 1, norm=True)
                group_in(2, 0)
                with pe.Fori(3, FT // 2 - 1, 2) as it:
                    group_in(it, 1)
                    group_in(it + 1, 0)
                tb = TILE_A[f] + 2 * FT
                for grp in range(2):
                    outs = [bank(4 * (1 - grp) + m) for m in range(4)]
                    for i in range(12):
                        ks = out_ks(i)

                        def before(m, i=i, ks=ks):
                            if i == 0:
                                pe.wait_ge(tile_read.h, tile_read.at(L, tb - 8 + 4 * grp + m + 1))
                            if m == 0 and grp == 0:
                                pe.wait_ge(h_lo.h, h_lo.at(L, f * FT + ks[-1] + 1))
                        chunk(L, 12 * grp + (CHUNK_A[f] + A_CHUNKS + i), i % RING, outs, ks, hhi, hlo, 0, FT, before)
                y_norm(L, 2 * f)

            def use(L, step, b):
                pe.wait_ge(misc_out[b].h, misc_out[b].at(L, USE[step, b]))

            def done(ins, b):
                ins.then_inc(misc[b].h, 1)

            def free_of_waits():
                pe.sem_inc(pe_begun.h, 1)

            def mixer(L):
                def got(step, b):
                    pe.wait_ge(misc_out[b].h, misc_out[b].at(L, USE[step, b] + 1))

                def half(v, a, i):
                    return v[CH * a:CH * a + CH, i, :]

                def do(step):
                    k = step[0]
                    if k == "xnorm":
                        x_stat(L, 1)
                        use(L, ("ba",), 5)
                        pe.wait_ge(ba_lo.h, ba_lo.at(L, 1))
                        for i in range(KT):
                            o, bh, bl = bank(5, 0, SEQ, 0, 8), bahi[:, i * 8:i * 8 + 8], balo[:, i * 8:i * 8 + 8]
                            pe.matmul(o, bh, uhi[:, i, :], start=i == 0, stop=False)
                            pe.matmul(o, bh, ulo[:, i, :], start=False, stop=False)
                            last = pe.matmul(o, bl, uhi[:, i, :], start=False, stop=i == KT - 1)
                        done(last, 5)
                        x_row(L, 1)
                    elif k == "bat":
                        use(L, step, 5)
                        for t in range(TT):
                            last = pe.matmul(bank(5, t * 8, 8), tmp[0:8, 2, t * P:(t + 1) * P], ident[0:8, 0:8], start=True, stop=True)
                        done(last, 5)
                    elif k == "gsum":
                        use(L, step, 5)
                        pe.wait_ge(g_dve.h, g_dve.at(L, 3))
                        for i, c in enumerate((K_TRI, K_STRICT, K_SELA, K_SELB)):
                            last = pe.matmul(bank(5, 16 * i, 16), con[:, c:c + P], g[:, :], start=True, stop=True)
                        done(last, 5)
                    elif k == "decay":
                        i = step[1]
                        use(L, step, 6 + i)
                        pe.wait_ge(gs_done.h, gs_done.at(L, 1))
                        free_of_waits()
                        for a in range(2):
                            q = slice(CH * a, CH * a + CH)
                            last = pe.matmul(ps[q, (6 + i) * SEQ:(7 + i) * SEQ], con[q, K_STRICT + CH * a:K_STRICT + CH * a + CH],
                                             Cs[q, 8 * i:8 * i + 8, :], start=True, stop=True)
                        done(last, 6 + i)
                    elif k in ("lst", "ost"):
                        w, h = (step[1], step[2]) if k == "lst" else (2, step[1])
                        if h == 0:
                            use(L, step, 5)
                        pe.wait_ge(l_sq.h, l_sq.at(L, 4 * w + h + 1))
                        stat(tmp[:, 2 + h % 2, :], bank(5, 4 * h, 4)).then_inc(l_stat.h, 1)
                        if h == 3:
                            pe.sem_inc(misc[5].h, 1)
                    elif k in ("row", "orow"):
                        w, h = (step[1], step[2]) if k == "row" else (2, step[1])
                        b = banks_of(step)[0]
                        use(L, step, b)
                        pe.wait_ge(rc_done.h, rc_done.at(L, STAT["kqo"[w]] + 1))
                        done(row(rc[:, 4 * h:4 * h + 4], bank(b)), b)
                    elif k in ("kk", "qk"):
                        i, b = step[1], banks_of(step)[0]
                        use(L, step, b)
                        if k == "kk":
                            for h in (2, 3):
                                got(("row", 0, h), 6 + h % 2)
                        else:
                            got(("row", 1, 3), 5)
                        for t in (2 * i, 2 * i + 1):
                            for h in range(H):
                                for a in range(2):
                                    c = slice(t * P + CH * a, t * P + CH * a + CH)
                                    last = pe.matmul(bank(b, ((t % 2) * H + h) * CH, CH, CH * a, CH * a + CH),
                                                     kq[:, 0, h, c], kq[:, int(k == "qk"), h, c], start=True, stop=True)
                        done(last, b)
                    elif k == "inv1":
                        i = step[1]
                        use(L, step, 6 + i)
                        pe.wait_ge(c_done.h, c_done.at(L, i + 1))
                        free_of_waits()
                        for c in range(8 * i, 8 * i + 8):
                            for a in range(2):
                                last = pe.matmul(bank(6 + i, (c % 8) * CH, CH, CH * a, CH * a + CH),
                                                 half(Cs, a, c), i64[CH * a:CH * a + CH, :], start=True, stop=True)
                        done(last, 6 + i)
                    elif k == "invp":
                        i, lev = step[1], step[2]
                        b = banks_of(step)[0]
                        use(L, step, b)
                        pe.wait_ge(c_done.h, c_done.at(L, 2 * lev + i + 1))
                        if lev == 1:
                            got(("inv1", i), 6 + i)
                        else:
                            got(("invd", i, lev - 1), banks_of(("invd", i, lev - 1))[1])
                        free_of_waits()
                        for c in range(8 * i, 8 * i + 8):
                            for a in range(2):
                                last = pe.matmul(bank(b, (c % 8) * 32, 32, CH * a, CH * a + CH),
                                                 half(Cs, a, c), block_cols(half(Zt, a, c), lev, 0), start=True, stop=True)
                        done(last, b)
                    elif k == "invd":
                        i, lev = step[1], step[2]
                        got(("invp", i, lev), banks_of(("invp", i, lev))[0])
                        for n, b in enumerate(banks_of(step)):
                            use(L, step, b)
                            free_of_waits()
                            for c in range(8 * i, 8 * i + 8):
                                for a in range(2):
                                    lh, rh = (Pm, Z) if n == 0 else (Z, Pm)
                                    last = pe.matmul(bank(b, (c % 8) * 32, 32, CH * a, CH * a + CH),
                                                     half(lh, a, c), block_cols(half(rh, a, c), lev, 1 - n), start=True, stop=True)
                            done(last, b)
                    elif k in ("ktr", "vtr"):
                        t, b = step[1], banks_of(step)[0]
                        use(L, step, b)
                        if k == "vtr":
                            pe.wait_ge(silu_done.h, silu_done.at(L, 8))
                        for h in range(H):
                            src = kq[:, 0, h, t * P:(t + 1) * P] if k == "ktr" else vT[:, h, t * P:(t + 1) * P]
                            last = pe.transpose(bank(b, h * P, P), src, ident)
                        done(last, b)
                    elif k == "rope":
                        i, b = step[1], banks_of(step)[0]
                        use(L, step, b)
                        pe.wait_ge(tile_read.h, tile_read.at(L, TILE_M + (16 if i < 4 else 17)))
                        done(pe.matmul(bank(b), con[:, K_ROT:K_ROT + P], attn_in(i), start=True, stop=True), b)
                    elif k == "vwin":
                        i = step[1]
                        use(L, step, 5)
                        pe.wait_ge(tile_read.h, tile_read.at(L, TILE_M + 18))
                        free_of_waits()
                        for n in range(4 * i, 4 * i + 4):
                            lo, w = (CH * (n - 1), P) if n else (0, CH)
                            last = pe.transpose(bank(5, (n % 4) * P, P, 0, w), sv[:, lo:lo + w], ident)
                        done(last, 5)
                    elif k == "grow":
                        h = step[1]
                        use(L, step, 6)
                        for t in range(TT):
                            last = pe.matmul(bank(6, t * P, P), g[:, 4 * t + h:4 * t + h + 1].to_broadcast([P, P]), tri,
                                             start=True, stop=True)
                        done(last, 6)
                    elif k == "wt":
                        t, b = step[1], banks_of(step)[0]
                        use(L, step, b)
                        if b == 4:
                            got(("invd", 0, LEVELS - 1), 7)
                        else:
                            got(("invd", 1, LEVELS - 1), 4)
                        free_of_waits()
                        for a in range(2):
                            q = slice(CH * a, CH * a + CH)
                            for h in range(H):
                                last = pe.matmul(bank(b, h * P + CH * a, CH), kte[q, t, h, :], Z[q, 4 * t + h, :],
                                                 start=True, stop=True)
                            if a == 0:
                                last.then_inc(w_half.h, 1)
                                pe.wait_ge(w_half.h, w_half.at(L, t + 1))
                                free_of_waits()
                        done(last, b)
                    elif k == "sc":
                        n = step[1]
                        lo, w = (CH * (n - 1), P) if n else (0, CH)
                        use(L, step, 5)
                        pe.wait_ge(roped.h, roped.at(L, 5))
                        for gg in range(2):
                            q = slice(CH * gg, CH * gg + CH)
                            for jp in range(2):
                                last = pe.matmul(bank(5, (2 * gg + jp) * P, w), sq[q, n, 2 * jp:2 * jp + 2, :].rearrange("p t c -> p (t c)"),
                                                 sk[q, lo:lo + w], start=True, stop=True)
                            if gg == 0:
                                last.then_inc(sc_half.h, 1)
                                pe.wait_ge(sc_half.h, sc_half.at(L, n + 1))
                        done(last, 5)
                    elif k == "pt":
                        n = step[1]
                        w = P if n else CH
                        use(L, step, 6)
                        pe.wait_ge(p_norm.h, p_norm.at(L, n + 1))
                        free_of_waits()
                        for b4 in range(4):
                            last = pe.transpose(bank(6, b4 * P, P, 0, w), pexp[:, b4, 0:w], ident)
                        done(last, 6)
                    elif k == "pv":
                        n = step[1]
                        w = P if n else CH
                        use(L, step, 7)
                        got(("pt", n), 6)
                        free_of_waits()
                        for gg in range(2):
                            for jp in range(2):
                                last = pe.matmul(bank(7, 256 + jp * P, P, CH * gg, CH * gg + CH), vwin[0:w, n, CH * gg:CH * gg + CH],
                                                 pT[0:w, 2 * gg + jp, :], start=True, stop=True)
                        done(last, 7)
                    elif k == "sv":
                        n = step[1]
                        t, a = n // 2, n % 2
                        q = slice(CH * a, CH * a + CH)
                        use(L, step, 4)
                        if n == 0:
                            got(("wt", 2), 4)
                            got(("wt", 3), 7)
                        else:
                            pe.wait_ge(s_new.h, s_new.at(L, n))
                        free_of_waits()
                        for h in range(H):
                            o = bank(4, h * P, P, CH * a, CH * a + CH)
                            last = pe.matmul(o, Z[q, 4 * t + h, :], vtm[q, t, h, :], start=True, stop=n == 0)
                            if n:
                                last = pe.matmul(o, wneg[:, h, CH * n:CH * n + CH], S[:, h, :], start=False, stop=True)
                        done(last, 4)
                    elif k == "so":
                        n = step[1]
                        t, a = n // 2, n % 2
                        q = slice(CH * a, CH * a + CH)
                        use(L, step, 7)
                        if n == 0:
                            pe.wait_ge(q_e.h, q_e.at(L, 4))
                            got(("qk", 0), 5)
                        got(("sv", n), 4)
                        free_of_waits()
                        for h in range(H):
                            o = bank(7, h * CH, CH)
                            if n:
                                pe.matmul(o, S[:, h, :], kq[:, 1, h, CH * n:CH * n + CH], start=True, stop=False)
                            last = pe.matmul(o, vn[q, h, :], attnT[q, 4 * t + h, :], start=n == 0, stop=True)
                        done(last, 7)
                        if n < NCH - 1:
                            use(L, step, 4)
                            for h in range(H):
                                last = pe.matmul(bank(4, h * P, P), ktl[q, t, h, :], vn[q, h, :], start=True, stop=True)
                            done(last, 4)

                tile = TILE_M
                for j in range(M_CHUNKS):
                    c = CHUNK_M + j
                    if j < 4:
                        first_chunk(L, c, j, [bank(m) for m in range(4)], 0, TILE_M - 8)
                    elif j < 40:
                        g0 = 16 if j in HALVES else 4 * (j // 4) if j < 16 else 18 + 4 * ((j - 20) // 4)
                        i = j % 4
                        nt = 2 if j in HALVES else 4

                        def before(m, j=j, i=i, g0=g0):
                            if i == 0:
                                prev = (g0 + m - 4 if g0 <= 16 else 14 + m if g0 == 18 and m > 1 else 16 + m if g0 == 18 else g0 + m - 4)
                                pe.wait_ge(tile_read.h, tile_read.at(L, TILE_M + prev + 1 if g0 else TILE_M - 8 + m + 1))
                                if g0 == 18 and m > 1:
                                    pe.wait_ge(misc_out[m].h, misc_out[m].at(L, USES[m]))
                        chunk(L, c, j % RING, [bank(m) for m in range(nt)], (2 * i, 2 * i + 1), uhi, ulo, 0, KT, before)
                    elif j < 48:
                        grp, i = (j - 40) // 2, j % 2
                        y = (ybhi, yblo) if grp < 2 else (yahi, yalo)

                        def before(m, grp=grp, i=i):
                            if i == 0:
                                pe.wait_ge(tile_read.h, tile_read.at(L, TILE_M + 38 + 4 * grp + m - 4 + 1))
                            if m == 0 and grp % 2 == 0:
                                pe.wait_ge(ys_lo.h, ys_lo.at(L, 4 * (grp // 2) + 2 * i + 2))
                        chunk(L, c, j % RING, [bank(m) for m in range(4)], (2 * i, 2 * i + 1), *y, 0, 4, before)
                    else:
                        grp, i = (j - 48) // 4, j % 4

                        def before(m, grp=grp, i=i):
                            if i == 0 and grp == 1:
                                pe.wait_ge(tile_read.h, tile_read.at(L, TILE_M + 50 + m + 1))
                            if i == 0 and grp == 0:
                                pe.wait_ge(misc_out[4 + m].h, misc_out[4 + m].at(L, USES[4 + m]))
                            if m == 0 and grp == 0:
                                pe.wait_ge(mg_lo.h, mg_lo.at(L, 2 * i + 2))
                        chunk(L, c, j % RING, [bank(4 * (1 - grp) + m) for m in range(4)], (2 * i, 2 * i + 1), uhi, ulo, 0, KT, before)
                    for step in MIX_STEPS[j]:
                        do(step)
                y_norm(L, 1)

            with pe.Fori(0, DEPTH) as L:
                ffn(L, 0)
                mixer(L)
                ffn(L, 1)

        @block.scalar
        def _(act):
            def split(s, slot_free, cols=1024):
                act.wait_ge(raw_ready[s].h, slot_free[0])
                act.wait_ge(gemm_done.h, slot_free[1])
                act.activation(whi[:, s, 0:cols], raw[:, s, 0:cols], ACT.Copy).then_inc(hi_done.h, 1)

            def turn(L, c4):
                return L * (LAYER_CHUNKS // RING * 16) + c4

            linked = [0]

            def link(L, ins):
                linked[0] += 1
                ins.then_inc(act_link.h, 1)
                act.wait_ge(act_link.h, act_link.at(L, linked[0]))

            def x_parts(L, n, k, gain, first=False):
                if not first:
                    act.wait_ge(x_new.h, x_new.at(L, 8 * n + k + 1))
                act.activation(uhi[:, k, :], x[:, k, :], ACT.Copy, scale=gain).then_inc(u_hi.h, 1)
                if k >= 2:
                    act.wait_ge(x_added.h, max(k - 2, 1) if first else x_added.at(L, 7 * n + max(k - 2, 1)))
                act.activation(tmp[:, k % 2, :], x[:, k, :], ACT.Square).then_inc(sq_done.h, 1)

            def y_squares(L, n, unit, ms_):
                for m in ms_:
                    r = (m + 4) % 8
                    act.wait_ge(gemm_done.h, gemm_done.at(L, unit + m % 4 + 1))
                    if r >= 2:
                        act.wait_ge(y_added.h, y_added.at(L, 7 * n + max(r - 2, 1)))
                    act.activation(tmp[:, m % 2, :], bank(m), ACT.Square).then_inc(sq_done.h, 1)
                    if m == 7:
                        act.activation(tmp[:, 3, :], bank(7), ACT.Copy).then_inc(y7_out.h, 1)

            def r_copy(L, name, scale):
                act.wait_ge(row_done.h, row_done.at(L, ROW[name] + 1))
                act.activation(rrow[:, :], bank(7), ACT.Copy, scale=scale).then_inc(r_ready.h, 1)

            def boundary(L, n, scale):
                r_copy(L, f"y{n}", scale)
                for k in range(KT):
                    gain = pc(L, G_MIXPRE + k) if n == 0 else pc(L, G_PRE[1] + k) if n == 1 else pc(L + 1, G_PRE[0] + k)
                    x_parts(L, n, k, gain)

            def group_out(L, f, it):
                for i in range(2):
                    act.wait_ge(tile_read.h, tile_read.at(L, it * 4 + (TILE_A[f] + 2 * i + 1)))
                    act.activation(tmp[:, 4 + i, :], tmp[:, i, :], ACT.Tanh, scale=0.5).then_inc(ff_tanh.h, 1)
                for i in range(2):
                    act.wait_ge(ff_h.h, ff_h.at(L, it * 2 + (f * FT + i + 1)))
                    act.activation(hhi[:, bass.ds(it * 2 + i, 1), :].rearrange("p a s -> p (a s)") if not isinstance(it, int)
                                   else hhi[:, 2 * it + i, :], tmp[:, 2 + i, :], ACT.Copy, scale=0.5).then_inc(h_hi.h, 1)

            def ffn(L, f):
                def slot(it, s):
                    s3 = (s + 3) % RING
                    t = (CHUNK_A[f] + s + 3) // RING
                    split(s3, (turn(L, it * 16 + 16 * (t + 1)), gemm_done.at(L, it * 16 + (UNIT_A[f] + 4 * s))))
                for s in range(4):
                    slot(0, s)
                r_copy(L, f"x{2 * f}", 1.0)
                group_out(L, f, 0)
                for it in (1, 2):
                    for s in range(4):
                        slot(it, s)
                    group_out(L, f, it)
                with act.Fori(3, FT // 2) as it:
                    for s in range(4):
                        slot(it, s)
                    group_out(L, f, it)
                ub = UNIT_A[f] + 4 * A_CHUNKS
                for i in range(24):
                    c = CHUNK_A[f] + A_CHUNKS + i
                    cols = 512 if i + 3 in (12, 13) else 1024
                    split((c + 3) % RING, (turn(L, 16 * ((c + 3) // RING + 1)), gemm_done.at(L, ub + 4 * i)), cols)
                    if i == 12:
                        y_squares(L, 2 * f, ub + 4 * 11, range(4, 8))
                y_squares(L, 2 * f, ub + 4 * 23, range(0, 4))
                boundary(L, 2 * f, 0.5)

            def mixer(L):
                def ready(step, b):
                    act.wait_ge(misc[b].h, misc[b].at(L, USE[step, b] + 1))

                def do(step):
                    k = step[0]
                    if k == "xnorm":
                        act.activation(bahi[:, :], pc(L, C_BA, 64), ACT.Copy).then_inc(ba_hi.h, 1)
                        act.activation(ealog[:, :], pc(L, C_ALOG, 4), ACT.Exp).then_inc(ea_done.h, 1)
                        r_copy(L, "x1", 1.0)
                    elif k == "conv":
                        i = step[1]
                        h = i % 4
                        act.wait_ge(tile_read.h, tile_read.at(L, TILE_M + i + 1))
                        if i == 0:
                            act.wait_ge(pad_zero.h, pad_zero.at(L, 1))
                        if i >= 2:
                            act.wait_ge(silu_done.h, silu_done.at(L, i - 1))
                        act.activation(tmp[:, 4 + i % 2, :], cv[:, h, 0:SEQ], ACT.Copy, scale=pc(L, C_CONV + 4 * i)).then_inc(tap0.h, 1)
                    elif k == "silu":
                        i = step[1]
                        act.wait_ge(conv_done.h, conv_done.at(L, i + 1))
                        act.activation(tmp[:, i % 2, :], tmp[:, 4 + i % 2, :], ACT.Tanh, scale=0.5).then_inc(c_tanh.h, 1)
                    elif k == "gprep":
                        act.wait_ge(g_dve.h, g_dve.at(L, 1))
                        link(L, act.activation(ga_t[:, :], gb_t[:, :], ACT.Abs))
                        link(L, act.activation(ga_t[:, :], ga_t[:, :], ACT.Exp, scale=-1.0))
                        for t in range(TT):
                            act.activation(beta[:, 4 * t:4 * t + 4], ba[:, 8 * t:8 * t + 4], ACT.Tanh, scale=0.5)
                        act.activation(ga_t[:, :], ga_t[:, :], ACT.Ln, bias=1.0).then_inc(g_act.h, 1)
                    elif k == "gsum":
                        ready(step, 5)
                        act.activation(exs[:, :], bank(5, 0, 64), ACT.Exp).then_inc(misc_out[5].h, 1)
                    elif k == "decay":
                        i = step[1]
                        ready(step, 6 + i)
                        act.activation(E[:, 8 * i:8 * i + 8, :], bank(6 + i).rearrange("p (a c) -> p a c", c=CH),
                                       ACT.Exp).then_inc(misc_out[6 + i].h, 1)
                    elif k in ("lst", "ost"):
                        w, h = (step[1], step[2]) if k == "lst" else (2, step[1])
                        n = 4 * w + h
                        if k == "lst":
                            act.wait_ge(silu_done.h, silu_done.at(L, 8 * w + h + 1))
                        if n >= 2:
                            act.wait_ge(l_stat.h, l_stat.at(L, n - 1))
                        src = kq[:, w, h, :] if k == "lst" else oT[:, h, :]
                        if k == "ost" and h == 0:
                            act.wait_ge(misc_out[7].h, misc_out[7].at(L, USE[("so", NCH - 1), 7] + 1))
                        act.activation(tmp[:, 2 + h % 2, :], src, ACT.Square, scale=0.5 if k == "lst" else 1.0).then_inc(l_sq.h, 1)
                    elif k == "invp":
                        i, lev, b = step[1], step[2], banks_of(step)[0]
                        ready(step, b)
                        act.wait_ge(p_zero.h, p_zero.at(L, 2 * (lev - 1) + i + 1))
                        act.activation(block_cols(Pm[:, 8 * i:8 * i + 8, :], lev, 0), half_cols(bank(b, 0, 256), lev),
                                       ACT.Copy).then_inc(misc_out[b].h, 1)
                    elif k == "vtr":
                        t = step[1]
                        ready(step, 7)
                        act.activation(vtm[:, t, :, :], bank(7).rearrange("p (h d) -> p h d", d=P), ACT.Copy,
                                       scale=0.5).then_inc(misc_out[7].h, 1)
                    elif k == "vwin":
                        i = step[1]
                        ready(step, 5)
                        if i == 0:
                            act.activation(vwin[0:CH, 0, :], bank(5, 0, P, 0, CH), ACT.Copy)
                            act.activation(vwin[:, 1:4, :], bank(5, P, 3 * P).rearrange("p (a c) -> p a c", c=P),
                                           ACT.Copy).then_inc(misc_out[5].h, 1)
                        else:
                            act.activation(vwin[:, 4:8, :], bank(5).rearrange("p (a c) -> p a c", c=P),
                                           ACT.Copy).then_inc(misc_out[5].h, 1)
                    elif k == "grow":
                        h = step[1]
                        ready(step, 6)
                        if h:
                            act.wait_ge(q_e.h, q_e.at(L, h))
                        act.activation(tmp[:, 0, :], bank(6), ACT.Exp).then_inc(misc_out[6].h, 1)
                    elif k == "wt":
                        t, b = step[1], banks_of(step)[0]
                        ready(step, b)
                        act.activation(wneg[:, :, t * P:(t + 1) * P], bank(b).rearrange("p (h c) -> p h c", c=P), ACT.Copy,
                                       scale=-1.0).then_inc(misc_out[b].h, 1)
                    elif k == "sc":
                        n = step[1]
                        w = P if n else CH
                        act.wait_ge(sc_max.h, sc_max.at(L, n + 1))
                        if n:
                            act.wait_ge(misc[6].h, misc[6].at(L, USE[("pt", n - 1), 6] + 1))
                        act.activation(es[:, 0:4], mneg[:, 4:8], ACT.Exp).then_inc(es_done.h, 1)
                        for b4 in range(4):
                            last = act.activation(pexp[:, b4, 0:w], bank(5, b4 * P, w), ACT.Exp, bias=mneg[:, b4:b4 + 1],
                                                  scale=SWA_SCALE, accum_out=sm[:, b4:b4 + 1])
                        last.then_inc(misc_out[5].h, 1)
                    elif k == "pt":
                        n = step[1]
                        w = P if n else CH
                        ready(step, 6)
                        if n:
                            act.wait_ge(misc[7].h, misc[7].at(L, USE[("pv", n - 1), 7] + 1))
                        act.activation(pT[0:w, :, :], bank(6, 0, SEQ, 0, w).rearrange("p (a c) -> p a c", c=P),
                                       ACT.Copy).then_inc(misc_out[6].h, 1)
                    elif k == "pv":
                        n = step[1]
                        ready(step, 7)
                        act.activation(yb[:, :, CH * n:CH * n + CH], bank(7, 256, 256).rearrange("p (t c) -> p t c", c=CH),
                                       ACT.Copy).then_inc(misc_out[7].h, 1)
                    elif k == "so":
                        n = step[1]
                        ready(step, 7)
                        act.activation(oT[:, :, CH * n:CH * n + CH], bank(7, 0, 256).rearrange("p (h c) -> p h c", c=CH),
                                       ACT.Copy).then_inc(misc_out[7].h, 1)
                    elif k == "zsilu":
                        i = step[1]
                        act.wait_ge(tile_read.h, tile_read.at(L, TILE_M + 18 + i + 1))
                        if i == 0:
                            act.wait_ge(q_e.h, q_e.at(L, 4))
                        if i >= 2:
                            act.wait_ge(z_done.h, z_done.at(L, i - 1))
                        act.activation(tmp[:, i % 2, :], z[:, i, :], ACT.Tanh, scale=0.5).then_inc(z_tanh.h, 1)
                    elif k == "evac" and 22 <= step[1] < 38:
                        i = step[1]
                        act.wait_ge(tile_read.h, tile_read.at(L, TILE_M + i + 1))
                        act.activation(gates[:, i - 22, :], tmp[:, 4 + i % 2, :], ACT.Tanh, scale=0.5).then_inc(gate_done.h, 1)
                    elif k == "ybs":
                        t = step[1]
                        if t == 0:
                            act.wait_ge(misc_out[7].h, misc_out[7].at(L, USE[("so", NCH - 1), 7] + 1))
                        act.activation(ybhi[:, t, :], yb[:, t, :], ACT.Copy).then_inc(ys_hi.h, 1)
                    elif k == "orow":
                        h = step[1]
                        act.wait_ge(o_done.h, o_done.at(L, h + 1))
                        act.activation(yahi[:, h, :], oT[:, h, :], ACT.Copy).then_inc(ys_hi.h, 1)
                    elif k == "evac" and step[1] >= 46:
                        i = step[1] - 46
                        act.wait_ge(mg_done.h, mg_done.at(L, i + 1))
                        act.activation(uhi[:, i, :], tmp[:, 4 + i % 2, :], ACT.Copy, scale=0.5).then_inc(mg_hi.h, 1)

                for j in range(M_CHUNKS):
                    c = CHUNK_M + j
                    split((c + 3) % RING, (turn(L, 16 * ((c + 3) // RING + 1)), gemm_done.at(L, m_unit(j))),
                          512 if j + 3 in HALVES else 1024)
                    for step in MIX_STEPS[j]:
                        do(step)
                    if j == 52:
                        y_squares(L, 1, m_unit(51), range(4, 8))
                y_squares(L, 1, m_unit(55), range(0, 4))
                boundary(L, 1, 1.0)

            act.wait_ge(par_in.h, 16)
            for k in range(KT):
                if k % 2 == 0:
                    act.wait_ge(x_in[k // 2].h, 16)
                x_parts(0, 0, k, prm[:, G_PRE[0] + k:G_PRE[0] + k + 1], first=True)
                if k % 2 == 0 and k < 6:
                    act.wait_ge(raw_ready[k // 2].h, 16)
                    act.activation(whi[:, k // 2, :], raw[:, k // 2, :], ACT.Copy).then_inc(hi_done.h, 1)
            with act.Fori(0, DEPTH) as L:
                ffn(L, 0)
                mixer(L)
                ffn(L, 1)
            assert linked[0] == ACT_LINKS, f"ACT_LINKS {linked[0]}"

        @block.vector
        def _(dve):
            dve.sem_inc(split_done.h, 4)
            dve.sem_inc(tile_read.h, 8)
            for b in USES:
                dve.sem_inc(misc_out[b].h, 1)
            linked = [0]

            def link(L, ins):
                linked[0] += 1
                ins.then_inc(dve_link.h, 1)
                dve.wait_ge(dve_link.h, dve_link.at(L, linked[0]))

            def split(L, c, s, cols=1024):
                dve.wait_ge(hi_done.h, hi_done.at(L, c + 1))
                dve.tensor_tensor(wlo[:, s, 0:cols], raw[:, s, 0:cols], whi[:, s, 0:cols].bitcast(f32), ALU.subtract) \
                   .then_inc(split_done.h, 1)

            def u_part(L, n, k, gain, first=False):
                dve.wait_ge(u_hi.h, k + 1 if first else u_hi.at(L, 8 * n + k + 1))
                dve.scalar_tensor_tensor(ulo[:, k, :], x[:, k, :], gain, uhi[:, k, :].bitcast(f32), ALU.mult, ALU.subtract) \
                   .then_inc(u_lo.h, 1)

            def y_sums(L, n, ms_):
                for m in ms_:
                    r = (m + 4) % 8
                    if r == 0:
                        continue
                    dve.wait_ge(sq_done.h, sq_done.at(L, 16 * n + r + 1))
                    if r > 1:
                        dve.wait_ge(y_added.h, y_added.at(L, 7 * n + r - 1))
                    dve.tensor_tensor(tmp[:, 2, :], tmp[:, 2 if r > 1 else 0, :], tmp[:, m % 2, :], ALU.add).then_inc(y_added.h, 1)

            def mean(L, name, src, cols, scale):
                dve.wait_ge(stat_done.h, stat_done.at(L, ROW[name] + 1))
                if STAT[name]:
                    dve.wait_ge(rc_done.h, rc_done.at(L, STAT[name]))
                dve.tensor_scalar(ms[:, 0:cols], src, scale, EPS, ALU.mult, ALU.add).then_inc(ms_done.h, 1)

            def boundary(L, n):
                mean(L, f"y{n}", bank(7, 0, 4), 4, 1.0 / D)
                dve.wait_ge(r_ready.h, r_ready.at(L, ROW[f"y{n}"] + 1))
                if n == 1:
                    dve.wait_ge(x_back.h, x_back.at(L, 16))
                post = (G_POST[0], G_MIXPOST, G_POST[1])[n]

                def gain(k):
                    return pc(L, G_MIXPRE + k) if n == 0 else pc(L, G_PRE[1] + k) if n == 1 else pc(L + 1, G_PRE[0] + k)
                for k in range(KT):
                    y = tmp[:, 3, :] if k == 7 else bank(k)
                    if k:
                        dve.wait_ge(x_new.h, x_new.at(L, 8 * n + k))
                    dve.scalar_tensor_tensor(tmp[:, 4, :], y, pc(L, post + k), rrow[:, :], ALU.mult, ALU.mult) \
                       .then_inc(tile_read.h, 1)
                    if k:
                        u_part(L, n, k - 1, gain(k - 1))
                    base = (TILE_A[0] + 2 * FT, TILE_M + 54, TILE_A[1] + 2 * FT)[n]
                    dve.wait_ge(tile_read.h, tile_read.at(L, base + k + 1))
                    dve.tensor_tensor(x[:, k, :], x[:, k, :], tmp[:, 4, :], ALU.add).then_inc(x_new.h, 1)
                u_part(L, n, KT - 1, gain(KT - 1))

            def group_out(L, f, it, odd):
                for i in range(2):
                    for w in range(2):
                        dve.wait_ge(gemm_done.h, gemm_done.at(L, it * 16 + (UNIT_A[f] + 12 + 2 * i + w + 1)))
                        dve.tensor_tensor(tmp[:, 2 * w + i, :], bank(4 * odd + 2 * i + w), rrow[:, :], ALU.mult).then_inc(tile_read.h, 1)
                for i in range(2):
                    dve.wait_ge(ff_tanh.h, ff_tanh.at(L, it * 2 + (f * FT + i + 1)))
                    dve.wait_ge(tile_read.h, tile_read.at(L, it * 4 + (TILE_A[f] + 4)))
                    dve.scalar_tensor_tensor(tmp[:, i, :], tmp[:, 4 + i, :], 1.0, tmp[:, i, :], ALU.add, ALU.mult).then_inc(ff_silu.h, 1)
                    dve.wait_ge(ff_silu.h, ff_silu.at(L, it * 2 + (f * FT + i + 1)))
                    dve.tensor_tensor(tmp[:, 2 + i, :], tmp[:, i, :], tmp[:, 2 + i, :], ALU.mult).then_inc(ff_h.h, 1)
                for i in range(2):
                    dve.wait_ge(h_hi.h, h_hi.at(L, it * 2 + (f * FT + i + 1)))
                    at_ = 2 * it + i if isinstance(it, int) else None
                    lo = hlo[:, at_, :] if at_ is not None else hlo[:, bass.ds(it * 2 + i, 1), :].rearrange("p a s -> p (a s)")
                    hi = hhi[:, at_, :] if at_ is not None else hhi[:, bass.ds(it * 2 + i, 1), :].rearrange("p a s -> p (a s)")
                    dve.scalar_tensor_tensor(lo, tmp[:, 2 + i, :], 0.5, hi.bitcast(f32), ALU.mult, ALU.subtract) \
                       .then_inc(h_lo.h, 1)

            def ffn(L, f):
                for s in range(4):
                    split(L, CHUNK_A[f] + s + 3, (s + 3) % RING)
                mean(L, f"x{2 * f}", bank(7, 0, 4), 4, 1.0 / D)
                dve.wait_ge(r_ready.h, r_ready.at(L, ROW[f"x{2 * f}"] + 1))
                group_out(L, f, 0, 0)

                def group(it, odd):
                    for s in range(4):
                        split(L, it * 4 + (CHUNK_A[f] + s + 3), (s + 3) % RING)
                    group_out(L, f, it, odd)

                group(1, 1)
                group(2, 0)
                with dve.Fori(3, FT // 2 - 1, 2) as it:
                    group(it, 1)
                    group(it + 1, 0)
                for i in range(24):
                    c = CHUNK_A[f] + A_CHUNKS + i
                    split(L, c + 3, (c + 3) % RING, 512 if i + 3 in (12, 13) else 1024)
                    if i == 12:
                        y_sums(L, 2 * f, range(4, 8))
                y_sums(L, 2 * f, range(0, 4))
                boundary(L, 2 * f)

            def mixer(L):
                def ready(step, b):
                    dve.wait_ge(misc[b].h, misc[b].at(L, USE[step, b] + 1))

                def got(step, b):
                    dve.wait_ge(misc_out[b].h, misc_out[b].at(L, USE[step, b] + 1))

                def cols(v, lo, n, w, p0=0, p1=P):
                    return v[p0:p1, lo:lo + n].rearrange("p (a c) -> p a c", c=1).to_broadcast([p1 - p0, n, w])

                def do(step):
                    k = step[0]
                    if k == "xnorm":
                        dve.wait_ge(ba_hi.h, ba_hi.at(L, 1))
                        dve.tensor_tensor(balo[:, :], pc(L, C_BA, 64), bahi[:, :].bitcast(f32), ALU.subtract).then_inc(ba_lo.h, 1)
                        mean(L, "x1", bank(7, 0, 4), 4, 1.0 / D)
                        dve.wait_ge(r_ready.h, r_ready.at(L, ROW["x1"] + 1))
                    elif k == "ba":
                        ready(step, 5)
                        dve.tensor_tensor(tmp[0:8, 2, :], bank(5, 0, SEQ, 0, 8), rrow[0:8, :], ALU.mult).then_inc(misc_out[5].h, 1)
                    elif k == "bat":
                        ready(step, 5)
                        dve.tensor_copy(ba[:, :], bank(5, 0, 32)).then_inc(misc_out[5].h, 1)
                    elif k == "gprep":
                        got(("bat",), 5)
                        bav = ba[:, :].rearrange("p (t c) -> p t c", c=8)
                        dt = pc(L, C_DT, 4).rearrange("p (a c) -> p a c", a=1).to_broadcast([P, TT, 4])
                        dve.tensor_tensor(gb_t[:, :].rearrange("p (t c) -> p t c", c=4), bav[:, :, 4:8], dt, ALU.add).then_inc(g_dve.h, 1)
                        dve.wait_ge(g_act.h, g_act.at(L, 1))
                        dve.wait_ge(ea_done.h, ea_done.at(L, 1))
                        dve.wait_ge(g_dve.h, g_dve.at(L, 1))
                        link(L, dve.scalar_tensor_tensor(gb_t[:, :], gb_t[:, :], 0.0, ga_t[:, :], ALU.max, ALU.add))
                        dve.tensor_scalar(beta[:, :], beta[:, :], 0.5, 0.5, ALU.mult, ALU.add).then_inc(g_dve.h, 1)
                        ea = ealog[:, :].rearrange("p (a c) -> p a c", a=1).to_broadcast([P, TT, 4])
                        dve.scalar_tensor_tensor(g[:, :].rearrange("p (t c) -> p t c", c=4), gb_t[:, :].rearrange("p (t c) -> p t c", c=4),
                                                 -1.0, ea, ALU.mult, ALU.mult).then_inc(g_dve.h, 1)
                        dve.wait_ge(g_dve.h, g_dve.at(L, 3))
                        dve.tensor_tensor(Cs[:, :, :], many(con[:, K_TRI64:K_TRI64 + 64], 16), cols(g, 0, 16, CH), ALU.mult) \
                           .then_inc(gs_done.h, 1)
                    elif k == "evac":
                        i = step[1]
                        b = (i if i < 18 else i - 18 if i < 38 else i - 38) % 4
                        j = 4 * (i // 4) + 3 if i < 16 else 19 if i < 18 else 4 * ((i - 18) // 4) + 23 if i < 38 else 2 * ((i - 38) // 4) + 41
                        m = i - 16 if 16 <= i < 18 else b
                        dve.wait_ge(gemm_done.h, gemm_done.at(L, m_unit(j) + m + 1))
                        if i < 38:
                            if i == 0:
                                dve.wait_ge(pad_zero.h, pad_zero.at(L, 1))
                            if i < 12:
                                if i >= 4:
                                    dve.wait_ge(conv_done.h, conv_done.at(L, i - 3))
                                dst = cv[:, i % 4, 3:3 + SEQ]
                            elif i < 16:
                                dve.wait_ge(conv_done.h, conv_done.at(L, 12))
                                dst = attn_in(i - 12)
                            elif i < 18:
                                dst = (sk, sv)[i - 16][:, :]
                            elif i < 22:
                                got(("invd", 0, LEVELS - 1), 7)
                                got(("invd", 1, LEVELS - 1), 4)
                                dst = z[:, i - 18, :]
                            else:
                                if i >= 24:
                                    dve.wait_ge(gate_done.h, gate_done.at(L, i - 23))
                                dst = tmp[:, 4 + i % 2, :]
                            src, by = bank(b), rrow[:, :]
                            if 12 <= i < 16:
                                src, by = chunks(src), chunks(by)
                            dve.tensor_tensor(dst, src, by, ALU.mult).then_inc(tile_read.h, 1)
                        elif i < 46:
                            i -= 38
                            dve.wait_ge(gate_done.h, gate_done.at(L, 16))
                            if i == 4:
                                dve.wait_ge(ys_lo.h, ys_lo.at(L, 4))
                            dve.scalar_tensor_tensor(m1[i // 4][:, i % 4, :], gates[:, 8 + i, :], 1.0, bank(b), ALU.add, ALU.mult) \
                               .then_inc(tile_read.h, 1)
                        else:
                            i -= 46
                            if i >= 2:
                                dve.wait_ge(mg_lo.h, mg_lo.at(L, i - 1))
                            dve.scalar_tensor_tensor(tmp[:, 4 + i % 2, :], gates[:, i, :], 1.0, bank(b), ALU.add, ALU.mult) \
                               .then_inc(tile_read.h, 1)
                            dve.wait_ge(tile_read.h, tile_read.at(L, TILE_M + 46 + i + 1))
                            dve.tensor_tensor(tmp[:, 4 + i % 2, :], tmp[:, 4 + i % 2, :], m1[i // 4][:, i % 4, :], ALU.add).then_inc(mg_done.h, 1)
                            dve.wait_ge(mg_hi.h, mg_hi.at(L, i + 1))
                            dve.scalar_tensor_tensor(ulo[:, i, :], tmp[:, 4 + i % 2, :], 0.5, uhi[:, i, :].bitcast(f32), ALU.mult,
                                                     ALU.subtract).then_inc(mg_lo.h, 1)
                    elif k == "conv":
                        i = step[1]
                        acc = tmp[:, 4 + i % 2, :]
                        dve.wait_ge(tap0.h, tap0.at(L, i + 1))
                        for n in (1, 2, 3):
                            ins = dve.scalar_tensor_tensor(acc, cv[:, i % 4, n:n + SEQ], pc(L, C_CONV + 4 * i + n), acc, ALU.mult, ALU.add)
                            if n < 3:
                                link(L, ins)
                            else:
                                ins.then_inc(conv_done.h, 1)
                    elif k == "silu":
                        i = step[1]
                        if i == 0:
                            dve.wait_ge(x_out.h, x_out.at(L, 16))
                        dst = kq[:, 0, i, :] if i < 4 else vT[:, i - 4, :] if i < 8 else kq[:, 1, i - 8, :]
                        dve.wait_ge(c_tanh.h, c_tanh.at(L, i + 1))
                        dve.scalar_tensor_tensor(dst, tmp[:, i % 2, :], 1.0, tmp[:, 4 + i % 2, :], ALU.add, ALU.mult) \
                           .then_inc(silu_done.h, 1)
                    elif k in ("lpow", "opow"):
                        w = step[1] if k == "lpow" else 2
                        dve.wait_ge(l_stat.h, l_stat.at(L, 4 * w + 4))
                        dve.wait_ge(rc_done.h, rc_done.at(L, STAT["kqo"[w]]))
                        dve.tensor_scalar(ms[:, 0:16], bank(5, 0, 16), 1.0 if w < 2 else 1.0 / P, EPS, ALU.mult, ALU.add) \
                           .then_inc(ms_done.h, 1)
                        dve.wait_ge(ms_done.h, ms_done.at(L, STAT["kqo"[w]] + 1))
                        dve.sem_inc(misc_out[5].h, 1)
                    elif k == "row":
                        w, h = step[1], step[2]
                        b = banks_of(step)[0]
                        ready(step, b)
                        dve.scalar_tensor_tensor(kq[:, w, h, :], kq[:, w, h, :], 0.5 if w == 0 else 0.5 * DK_SCALE, bank(b),
                                                 ALU.mult, ALU.mult).then_inc(misc_out[b].h, 1)
                    elif k in ("kk", "qk"):
                        i, b = step[1], banks_of(step)[0]
                        src, dst = (N, N) if k == "kk" else (E, attnT)
                        dve.wait_ge(dmask.h, dmask.at(L, 1 if k == "kk" else 2))
                        ready(step, b)
                        dve.tensor_tensor(dst[:, 8 * i:8 * i + 8, :], src[:, 8 * i:8 * i + 8, :],
                                          bank(b).rearrange("p (a c) -> p a c", c=CH), ALU.mult).then_inc(misc_out[b].h, 1)
                    elif k == "inv1":
                        i = step[1]
                        s8 = slice(8 * i, 8 * i + 8)
                        dve.wait_ge(c_done.h, c_done.at(L, i + 1))
                        dve.tensor_tensor(Z[:, s8, :], many(i64, 8), Cs[:, s8, :], ALU.subtract).then_inc(z1_done.h, 1)
                        ready(step, 6 + i)
                        dve.tensor_tensor(Zt[:, s8, :], many(i64, 8), bank(6 + i).rearrange("p (a c) -> p a c", c=CH),
                                          ALU.subtract).then_inc(misc_out[6 + i].h, 1)
                    elif k == "invd":
                        i, lev = step[1], step[2]
                        s8 = slice(8 * i, 8 * i + 8)
                        if lev == 1:
                            dve.wait_ge(z1_done.h, z1_done.at(L, i + 1))
                            got(("inv1", i), 6 + i)
                        else:
                            got(("invd", i, lev - 1), banks_of(("invd", i, lev - 1))[0])
                            got(("invd", i, lev - 1), banks_of(("invd", i, lev - 1))[1])
                        bs = banks_of(step)
                        for b in bs:
                            ready(step, b)
                        for odd, v, b in zip((1, 0), (Z, Zt), bs):
                            part = block_cols(v[:, s8, :], lev, odd)
                            dve.tensor_tensor(part, part, half_cols(bank(b, 0, 256), lev), ALU.subtract).then_inc(misc_out[b].h, 1)
                    elif k == "ktr":
                        t, b = step[1], banks_of(step)[0]
                        ready(step, b)
                        got(("gsum",), 5)
                        src = bank(b).rearrange("p (h d) -> p h d", d=P)
                        dve.tensor_tensor(kte[:, t, :, :], src, cols(exs, 4 * t, 4, P), ALU.mult)
                        dve.tensor_tensor(ktl[:, t, :, :], src, cols(exs, 16 + 4 * t, 4, P), ALU.mult).then_inc(misc_out[b].h, 1)
                    elif k == "rope":
                        i, b = step[1], banks_of(step)[0]
                        ready(step, b)
                        dve.wait_ge(rope_in.h, rope_in.at(L, 16))
                        link(L, dve.tensor_tensor(tmp[:, 2 + i % 2, :], bank(b), rcs[:, 1, :], ALU.mult))
                        dve.wait_ge(rot_cos.h, rot_cos.at(L, i + 1))
                        dve.tensor_tensor(attn_in(i), chunks(tmp[:, 2 + i % 2, :]), chunks(tmp[:, i % 2, :]), ALU.add).then_inc(roped.h, 1)
                        dve.wait_ge(roped.h, roped.at(L, i + 1))
                        dve.sem_inc(misc_out[b].h, 1)
                    elif k == "grow":
                        h = step[1]
                        got(step, 6)
                        got(("row", 1, 3), 5)
                        dve.tensor_tensor(kq[:, 1, h, :], kq[:, 1, h, :], tmp[:, 0, :], ALU.mult).then_inc(q_e.h, 1)
                    elif k == "sc":
                        n = step[1]
                        w = P if n else CH
                        ready(step, 5)
                        link(L, dve.reduce_max(mx[:, 0:4], bank(5).rearrange("p (a c) -> p a c", c=P)[:, :, 0:w], AX.X))
                        link(L, dve.scalar_tensor_tensor(mx[:, 4:8], mx[:, 0:4], SWA_SCALE, pc(L, C_SINK, 4), ALU.mult, ALU.max))
                        link(L, dve.tensor_scalar(mneg[:, 0:4], mx[:, 4:8], -1.0, None, ALU.mult))
                        dve.tensor_tensor(mneg[:, 4:8], pc(L, C_SINK, 4), mneg[:, 0:4], ALU.add).then_inc(sc_max.h, 1)
                        dve.wait_ge(es_done.h, es_done.at(L, n + 1))
                        got(step, 5)
                        link(L, dve.tensor_tensor(rden[:, 0:4], sm[:, 0:4], es[:, 0:4], ALU.add))
                        link(L, dve.reciprocal(rden[:, 4:8], rden[:, 0:4]))
                        dve.tensor_tensor(pexp[:, :, 0:w], pexp[:, :, 0:w], cols(rden, 4, 4, w), ALU.mult).then_inc(p_norm.h, 1)
                    elif k == "sv":
                        n = step[1]
                        t, a = n // 2, n % 2
                        ready(step, 4)
                        dve.tensor_tensor(vn[CH * a:CH * a + CH, :, :], bank(4, 0, SEQ, CH * a, CH * a + CH).rearrange("p (h d) -> p h d", d=P),
                                          cols(beta, 4 * t, 4, P, CH * a, CH * a + CH), ALU.mult).then_inc(misc_out[4].h, 1)
                    elif k == "so" and step[1] < NCH - 1:
                        n = step[1]
                        t, a = n // 2, n % 2
                        ready(step, 4)
                        for h in range(H):
                            src = bank(4, h * P, P)
                            if n == 0:
                                last = dve.tensor_copy(S[:, h, :], src)
                            else:
                                if h == 0:
                                    dve.wait_ge(s_new.h, s_new.at(L, n))
                                c = 32 + 16 * a + 4 * t + h
                                last = dve.scalar_tensor_tensor(S[:, h, :], S[:, h, :], exs[:, c:c + 1], src, ALU.mult, ALU.add)
                        last.then_inc(s_new.h, 1)
                        dve.wait_ge(s_new.h, s_new.at(L, n + 1))
                        dve.sem_inc(misc_out[4].h, 1)
                    elif k == "zsilu":
                        i = step[1]
                        dve.wait_ge(z_tanh.h, z_tanh.at(L, i + 1))
                        dve.scalar_tensor_tensor(z[:, i, :], tmp[:, i % 2, :], 1.0, z[:, i, :], ALU.add, ALU.mult).then_inc(z_done.h, 1)
                    elif k == "ybs":
                        t = step[1]
                        dve.wait_ge(ys_hi.h, ys_hi.at(L, t + 1))
                        dve.tensor_tensor(yblo[:, t, :], yb[:, t, :], ybhi[:, t, :].bitcast(f32), ALU.subtract).then_inc(ys_lo.h, 1)
                    elif k == "orow":
                        h, b = step[1], banks_of(step)[0]
                        ready(step, b)
                        dve.scalar_tensor_tensor(oT[:, h, :], oT[:, h, :], pc(L, C_ONORM), bank(b), ALU.mult, ALU.mult) \
                           .then_inc(misc_out[b].h, 1)
                        got(step, b)
                        dve.wait_ge(z_done.h, z_done.at(L, 4))
                        dve.scalar_tensor_tensor(oT[:, h, :], oT[:, h, :], 0.5, z[:, h, :], ALU.mult, ALU.mult).then_inc(o_done.h, 1)
                        dve.wait_ge(ys_hi.h, ys_hi.at(L, 4 + h + 1))
                        dve.tensor_tensor(yalo[:, h, :], oT[:, h, :], yahi[:, h, :].bitcast(f32), ALU.subtract).then_inc(ys_lo.h, 1)

                for j in range(M_CHUNKS):
                    c = CHUNK_M + j
                    split(L, c + 3, (c + 3) % RING, 512 if j + 3 in HALVES else 1024)
                    for step in MIX_STEPS[j]:
                        do(step)
                    if j == 52:
                        y_sums(L, 1, range(4, 8))
                y_sums(L, 1, range(0, 4))
                boundary(L, 1)

            dve.wait_ge(par_in.h, 16)
            for k in range(KT):
                if k % 2 == 0:
                    dve.wait_ge(x_in[k // 2].h, 16)
                u_part(0, 0, k, prm[:, G_PRE[0] + k:G_PRE[0] + k + 1], first=True)
                if k % 2 == 0 and k < 6:
                    dve.wait_ge(hi_done.h, k // 2 + 1)
                    dve.tensor_tensor(wlo[:, k // 2, :], raw[:, k // 2, :], whi[:, k // 2, :].bitcast(f32), ALU.subtract) \
                       .then_inc(split_done.h, 1)
            dve.wait_ge(con_in.h, 16)
            with dve.Fori(0, DEPTH) as L:
                ffn(L, 0)
                mixer(L)
                ffn(L, 1)
            assert linked[0] == DVE_LINKS, f"DVE_LINKS {linked[0]}"

        @block.gpsimd
        def _(pool):
            pool.memset(neghalf[:, :], -0.5).then_inc(prepared.h, 1)
            pool.wait_ge(prepared.h, 1)
            linked = [0]

            def x_sums(L, n, first=False):
                for k in range(1, KT):
                    pool.wait_ge(sq_done.h, k + 1 if first else sq_done.at(L, 16 * n + 8 + k + 1))
                    if k > 1:
                        pool.wait_ge(x_added.h, k - 1 if first else x_added.at(L, 7 * n + k - 1))
                    pool.tensor_tensor(tmp[:, 5, :], tmp[:, 5 if k > 1 else 0, :], tmp[:, k % 2, :], ALU.add).then_inc(x_added.h, 1)

            def power(L, name, dst, cols):
                pool.wait_ge(ms_done.h, ms_done.at(L, STAT[name] + 1))
                pool.tensor_tensor(dst[:, 0:cols], ms[:, 0:cols], neghalf[:, 0:cols], ALU.pow).then_inc(rc_done.h, 1)

            def mixer(L):
                def do(step):
                    k = step[0]
                    if k == "xnorm":
                        power(L, "x1", rcx, 4)
                    elif k == "lpow":
                        if step[1] == 1:
                            pool.wait_ge(misc[7].h, misc[7].at(L, USE[("row", 0, 3), 7] + 1))
                        power(L, "kq"[step[1]], rc, 16)
                    elif k == "opow":
                        power(L, "o", rc, 16)
                    elif k == "decay" and step[1] == 1:
                        for i in range(2):
                            pool.wait_ge(misc_out[6 + i].h, misc_out[6 + i].at(L, USE[("decay", i), 6 + i] + 1))
                        pool.wait_ge(g_dve.h, g_dve.at(L, 2))
                        pool.tensor_tensor(N[:, :, :], E[:, :, :], many(con[:, K_STR64:K_STR64 + 64], 16), ALU.mult).then_inc(pool_link.h, 1)
                        pool.wait_ge(pool_link.h, pool_link.at(L, 1))
                        pool.tensor_tensor(N[:, :, :], N[:, :, :], beta[:, :].rearrange("p (a c) -> p a c", c=1).to_broadcast([P, 16, CH]),
                                           ALU.mult).then_inc(dmask.h, 1)
                        pool.tensor_tensor(E[:, :, :], E[:, :, :], many(con[:, K_TRI64:K_TRI64 + 64], 16), ALU.mult).then_inc(dmask.h, 1)
                    elif k in ("inv1", "invp"):
                        i, lev = step[1], 0 if k == "inv1" else step[2]
                        s8 = slice(8 * i, 8 * i + 8)
                        if lev == 0:
                            b = banks_of(("kk", i))[0]
                            pool.wait_ge(misc_out[b].h, misc_out[b].at(L, USE[("kk", i), b] + 1))
                        else:
                            b = 6 + i if lev == 1 else banks_of(("invp", i, lev - 1))[0]
                            last = ("inv1", i) if lev == 1 else ("invp", i, lev - 1)
                            pool.wait_ge(misc[b].h, misc[b].at(L, USE[last, b] + 1))
                            if lev == 1:
                                pool.wait_ge(z1_done.h, z1_done.at(L, i + 1))
                        pool.tensor_tensor(Cs[:, s8, :], N[:, s8, :], many(con[:, K_LEV + 64 * lev:K_LEV + 64 * lev + 64], 8),
                                           ALU.mult).then_inc(c_done.h, 1)
                        if lev > 1:
                            used = ("invd", i, lev - 1)
                            pool.wait_ge(misc[banks_of(used)[1]].h, misc[banks_of(used)[1]].at(L, USE[used, banks_of(used)[1]] + 1))
                            pool.sem_inc(pool_begun.h, 1)
                        if lev:
                            pool.memset(Pm[:, s8, :], 0.0).then_inc(p_zero.h, 1)
                    elif k == "rope":
                        i = step[1]
                        if i == 0:
                            pool.wait_ge(rope_in.h, rope_in.at(L, 16))
                            pool.wait_ge(silu_done.h, silu_done.at(L, 12))
                        if i >= 2:
                            pool.wait_ge(roped.h, roped.at(L, i - 1))
                        pool.wait_ge(tile_read.h, tile_read.at(L, TILE_M + (12 + i if i < 4 else 16) + 1))
                        pool.tensor_tensor(chunks(tmp[:, i % 2, :]), attn_in(i), chunks(rcs[:, 0, :]), ALU.mult).then_inc(rot_cos.h, 1)

                pool.wait_ge(u_lo.h, u_lo.at(L, 8))
                pool.sem_inc(pool_begun.h, 1)
                pool.dma_start(x_home, x[:, :, :]).then_inc(x_out.h, 16)
                pool.dma_start(rcs[:, :, :], rope).then_inc(rope_in.h, 16)
                pool.memset(cv[:, :, 0:3], 0.0).then_inc(pad_zero.h, 1)
                for j in range(M_CHUNKS):
                    for step in MIX_STEPS[j]:
                        do(step)
                    if j == 47:
                        pool.wait_ge(mg_done.h, mg_done.at(L, 8))
                        pool.wait_ge(gemm_done.h, gemm_done.at(L, m_unit(44)))
                        pool.wait_ge(x_out.h, x_out.at(L, 16))
                        pool.sem_inc(pool_begun.h, 1)
                        pool.dma_start(x[:, :, :], x_home).then_inc(x_back.h, 16)
                power(L, "y1", rc, 4)
                x_sums(L, 1)

            x_sums(0, 0, first=True)
            with pool.Fori(0, DEPTH) as L:
                power(L, "x0", rcx, 4)
                power(L, "y0", rc, 4)
                x_sums(L, 0)
                mixer(L)
                power(L, "x2", rcx, 4)
                power(L, "y2", rc, 4)
                x_sums(L, 2)


DVE_LINKS = 70
ACT_LINKS = 2
POOL_LINKS = 1


def constants():
    import numpy as np
    i = np.arange(P)
    same = (i[:, None] // CH) == (i[None, :] // CH)
    c = np.zeros((P, NCONST), np.float32)
    c[:, K_ID:K_ID + P] = np.eye(P)
    c[:, K_ONE:K_ONE + P] = 1.0
    c[:, K_TRI:K_TRI + P] = same & (i[:, None] <= i[None, :])
    c[:, K_STRICT:K_STRICT + P] = same & (i[:, None] > i[None, :])
    half = CH // 2
    for m in range(P):
        d = m % CH
        c[m + half if d < half else m - half, K_ROT + m] = -1.0 if d < half else 1.0
    c[:CH, K_SELA:K_SELA + P] = 1.0
    c[CH:, K_SELB:K_SELB + P] = 1.0
    r, q = (i % CH)[:, None], np.arange(CH)[None, :]
    c[:, K_I64:K_I64 + 64] = r == q
    c[:, K_TRI64:K_TRI64 + 64] = r <= q
    c[:, K_STR64:K_STR64 + 64] = r < q
    for lev in range(LEVELS):
        s = 1 << lev
        c[:, K_LEV + 64 * lev:K_LEV + 64 * lev + 64] = (r // (2 * s) == q // (2 * s)) & (r % (2 * s) < s) & (q % (2 * s) >= s)
    inv = np.float32(10000.0) ** (-np.arange(half, dtype=np.float32) / np.float32(half))
    ang = np.arange(SEQ, dtype=np.float32)[None, :] * inv.astype(np.float32)[:, None]
    rope = np.stack([np.tile(np.cos(ang), (4, 1)), np.tile(np.sin(ang), (4, 1))], 1)
    return c, np.ascontiguousarray(rope.astype(np.float32))


def lay_out(a):
    import numpy as np
    ws = np.zeros((DEPTH * LAYER_CHUNKS + 3, P, 1024), np.float32)
    par = np.zeros((P, (DEPTH + 1) * NPAR), np.float32)
    heads = [np.r_[CH * t:CH * t + CH, CH * (t + 4):CH * (t + 4) + CH] for t in range(4)]
    for l in range(DEPTH):
        c = [l * LAYER_CHUNKS]

        def put(w, k, tiles):
            b = np.stack([w[P * kk:P * kk + P, t] for kk in k for t in tiles], 1)
            ws[c[0], :, :b.shape[1] * P] = b.reshape(P, -1)
            c[0] += 1

        def ffn(w_in, w_out):
            for g in range(FT // 2):
                tiles = [np.arange(o + P * (2 * g + i), o + P * (2 * g + i) + P) for i in range(2) for o in (0, FF)]
                for s in range(4):
                    put(w_in, (2 * s, 2 * s + 1), tiles)
            for g in range(2):
                tiles = cols(512 * (1 - g), 4)
                for i in range(12):
                    put(w_out, out_ks(i), tiles)

        def cols(o, n):
            return [np.arange(o + P * m, o + P * m + P) for m in range(n)]

        ffn(a["ffn1_w_in"][l], a["ffn1_w_out"][l])
        w = a["mix_w_in"][l]
        swaq = [2056 + h for h in heads]
        groups = [cols(512, 4), cols(1024, 4), cols(0, 4), swaq, cols(2568, 2), cols(1536, 4)]
        groups += [cols(2824 + 512 * i, 4) for i in range(4)]
        for tiles in groups:
            for s in range(4):
                put(w, (2 * s, 2 * s + 1), tiles)
        wb = a["w_branch_b"][l][np.concatenate(heads)]
        for br in (wb, a["w_branch_a"][l]):
            for g in range(2):
                for s in range(2):
                    put(br, (2 * s, 2 * s + 1), cols(512 * g, 4))
        for g in range(2):
            for s in range(4):
                put(a["mix_w_out"][l], (2 * s, 2 * s + 1), cols(512 * (1 - g), 4))
        ffn(a["ffn2_w_in"][l], a["ffn2_w_out"][l])
        assert c[0] == (l + 1) * LAYER_CHUNKS
        p = par[:, l * NPAR:(l + 1) * NPAR]
        for o, name in ((G_PRE[0], "ffn1_pre_norm"), (G_POST[0], "ffn1_post_norm"), (G_PRE[1], "ffn2_pre_norm"),
                        (G_POST[1], "ffn2_post_norm"), (G_MIXPRE, "mix_pre_norm"), (G_MIXPOST, "mix_post_norm")):
            p[:, o:o + KT] = a[name][l].reshape(KT, P).T
        conv = a["dn_conv_w"][l]
        for i in range(12):
            o = (512, 1024, 0)[i // 4] + P * (i % 4)
            p[:, C_CONV + 4 * i:C_CONV + 4 * i + 4] = conv[:, o:o + P].T
        p[:, C_ONORM] = a["dn_out_norm"][l]
        p[:, C_ALOG:C_ALOG + 4] = a["dn_a_log"][l]
        p[:, C_DT:C_DT + 4] = a["dn_dt_bias"][l]
        for gg in range(2):
            for jp in range(2):
                for hh in range(2):
                    p[CH * hh:CH * hh + CH, C_SINK + 2 * gg + jp] = a["swa_sinks"][l][4 * gg + 2 * jp + hh]
        p[:, C_BA:C_BA + 64] = w[:, 2048:2056].reshape(KT, P, 8).transpose(1, 0, 2).reshape(P, 64)
    return ws, par


def kernel(**inputs):
    import numpy as _np
    import concourse.bacc as _bacc
    from concourse import mybir as _mybir
    from concourse.bass_utils import run_bass_kernel_spmd as _run

    a = {k: _np.asarray(v) for k, v in inputs.items()}
    ws, par = lay_out(a)
    con, rope = constants()
    xT = _np.ascontiguousarray(a["x"][0].T.reshape(KT, P, SEQ).transpose(1, 0, 2))
    nc = _bacc.Bacc("TRN2", target_bir_lowering=False, num_devices=1)
    arrays, args = {}, []
    for name, v in (("wstream", ws), ("xT", xT), ("par", par), ("con", con), ("rope", rope)):
        arrays[f"in_{name}_dram"] = v
        args.append(nc.dram_tensor(f"in_{name}_dram", v.shape, _mybir.dt.from_np(v.dtype), kind="ExternalInput").ap())
    args.append(nc.dram_tensor("out_0_dram", (P, KT, SEQ), _mybir.dt.float32, kind="ExternalOutput").ap())
    trunk(nc, *args)
    r = _run(nc, [arrays], core_ids=[0])
    got = r.results[0]["out_0_dram"]
    return _np.ascontiguousarray(got.transpose(1, 0, 2).reshape(D, SEQ).T)[None]
```
